# Optimizing a Trainium2 kernel written in Bass

```python
import math
import jax, jax.numpy as jnp
from jax import lax
import numpy as np

D_MODEL = 1024
BATCH = 1
SEQ = 1024
DEPTH = 1

D_MIX = D_MODEL
RET_WIDTH = D_MIX // 2
RET_HEADS = 4
RET_HEAD_DIM = RET_WIDTH // RET_HEADS
RET_CHUNK = 128
ROPE_BASE = 10000.0
SSM_WIDTH = D_MIX - RET_WIDTH
SSM_GROUP = 16
SSM_GROUPS = SSM_WIDTH // SSM_GROUP
SSM_STATE = 64
DT_MIN = 1e-3
DT_MAX = 1e-1
D_FF = 4 * D_MODEL
NORM_EPS = 1e-6
IN_COLS = 4 * RET_WIDTH + SSM_WIDTH


def rmsnorm(x, g):
    xf = x.astype(jnp.float32)
    y = xf * lax.rsqrt(jnp.mean(xf * xf, axis=-1, keepdims=True) + NORM_EPS) * g.astype(jnp.float32)
    return y.astype(x.dtype)

def rope(x):
    L, d = x.shape[1], x.shape[-1]
    half = d // 2
    inv_freq = ROPE_BASE ** (-jnp.arange(half, dtype=jnp.float32) / half)
    ang = jnp.arange(L, dtype=jnp.float32)[:, None] * inv_freq[None, :]
    cos = jnp.cos(ang)[None, :, None, :]
    sin = jnp.sin(ang)[None, :, None, :]
    x1, x2 = x[..., :half], x[..., half:]
    return jnp.concatenate([x1 * cos - x2 * sin, x1 * sin + x2 * cos], axis=-1)

def retention_chunkwise(q, k, v):
    B, L, H, d = q.shape
    C = RET_CHUNK
    nc = L // C
    log_gamma = jnp.log(1.0 - jnp.exp(jnp.linspace(math.log(1.0 / 32), math.log(1.0 / 512), H))).astype(jnp.float32)
    q = q.reshape(B, nc, C, H, d)
    k = k.reshape(B, nc, C, H, d)
    v = v.reshape(B, nc, C, H, d)
    idx = jnp.arange(C, dtype=jnp.float32)
    diff = idx[:, None] - idx[None, :]
    decay = jnp.where(diff[None] >= 0, jnp.exp(jnp.maximum(diff, 0.0)[None] * log_gamma[:, None, None]), 0.0)
    s = jnp.einsum('bnihk,bnjhk->bnhij', q, k) * decay[None, None]
    inner = jnp.einsum('bnhij,bnjhd->bnihd', s, v)
    zeta = jnp.exp((C - 1 - idx)[None, :] * log_gamma[:, None])
    S = jnp.einsum('bnjhk,bnjhd,hj->bnhkd', k, v, zeta)
    g_chunk = jnp.exp(C * log_gamma)[None, :, None, None]

    def step(R, S_i):
        return g_chunk * R + S_i, R

    R0 = jnp.zeros((B, H, d, d), jnp.float32)
    _, R_prev = lax.scan(step, R0, jnp.moveaxis(S, 1, 0))
    R_prev = jnp.moveaxis(R_prev, 0, 1)
    xi = jnp.exp((idx + 1.0)[None, :] * log_gamma[:, None])
    cross = jnp.einsum('bnihk,bnhkd,hi->bnihd', q, R_prev, xi)
    return (inner + cross).reshape(B, L, H, d)

def head_groupnorm(y, g):
    mu = jnp.mean(y, axis=-1, keepdims=True)
    var = jnp.mean(jnp.square(y - mu), axis=-1, keepdims=True)
    yn = (y - mu) * lax.rsqrt(var + NORM_EPS)
    return yn * g.astype(jnp.float32).reshape(RET_HEADS, RET_HEAD_DIM)

def s5_scan(u, lam_re, lam_im, log_dt, b_re, b_im, c_re, c_im, d_skip):
    B, L, _ = u.shape
    uf = u.astype(jnp.float32).reshape(B, L, SSM_GROUPS, SSM_GROUP)
    lam = lax.complex(jnp.minimum(lam_re.astype(jnp.float32), -1e-4), lam_im.astype(jnp.float32))
    dt = jnp.exp(log_dt.astype(jnp.float32))[:, None]
    lam_bar = jnp.exp(lam * dt)
    b_c = lax.complex(b_re.astype(jnp.float32), b_im.astype(jnp.float32))
    b_bar = ((lam_bar - 1.0) / lam)[:, :, None] * b_c
    bu = jnp.einsum('blgc,gpc->blgp', uf.astype(jnp.complex64), b_bar)
    a = jnp.broadcast_to(lam_bar, bu.shape)

    def combine(e1, e2):
        a1, x1 = e1
        a2, x2 = e2
        return a2 * a1, a2 * x1 + x2

    _, states = lax.associative_scan(combine, (a, bu), axis=1)
    c_c = lax.complex(c_re.astype(jnp.float32), c_im.astype(jnp.float32))
    y = jnp.real(jnp.einsum('blgp,gcp->blgc', states, c_c))
    y = y + d_skip.astype(jnp.float32).reshape(SSM_GROUPS, SSM_GROUP) * uf
    return y.reshape(B, L, SSM_WIDTH)

def first_inputs(seed: int = 0) -> dict:
    key = jax.random.key(seed)
    ks = jax.random.split(key, 20)
    f32 = jnp.float32
    nrm = lambda k, shape, scale: (jax.random.normal(k, shape, f32) * scale)
    gain = lambda k, shape: 1.0 + 0.02 * jax.random.normal(k, shape, f32)
    x = jax.random.normal(ks[0], (BATCH, SEQ, D_MODEL), f32)
    lam_im_base = math.pi * jnp.arange(SSM_STATE, dtype=f32)
    return {
        "x": x,
        "norm_mix_pre": gain(ks[1], (DEPTH, D_MODEL)),
        "norm_mix_post": gain(ks[2], (DEPTH, D_MODEL)),
        "w_in": nrm(ks[3], (DEPTH, D_MODEL, IN_COLS), D_MODEL ** -0.5),
        "ret_gn_gain": gain(ks[4], (DEPTH, RET_WIDTH)),
        "ssm_lambda_re": -0.5 + 0.01 * jax.random.normal(ks[5], (DEPTH, SSM_GROUPS, SSM_STATE), f32),
        "ssm_lambda_im": lam_im_base + 0.01 * jax.random.normal(ks[6], (DEPTH, SSM_GROUPS, SSM_STATE), f32),
        "ssm_log_dt": jax.random.uniform(ks[7], (DEPTH, SSM_GROUPS), f32, math.log(DT_MIN), math.log(DT_MAX)),
        "ssm_b_re": nrm(ks[8], (DEPTH, SSM_GROUPS, SSM_STATE, SSM_GROUP), (2 * SSM_GROUP) ** -0.5),
        "ssm_b_im": nrm(ks[9], (DEPTH, SSM_GROUPS, SSM_STATE, SSM_GROUP), (2 * SSM_GROUP) ** -0.5),
        "ssm_c_re": nrm(ks[10], (DEPTH, SSM_GROUPS, SSM_GROUP, SSM_STATE), (2 * SSM_STATE) ** -0.5),
        "ssm_c_im": nrm(ks[11], (DEPTH, SSM_GROUPS, SSM_GROUP, SSM_STATE), (2 * SSM_STATE) ** -0.5),
        "ssm_d": nrm(ks[12], (DEPTH, SSM_WIDTH), 1.0),
        "w_glu": nrm(ks[13], (DEPTH, SSM_WIDTH, 2 * SSM_WIDTH), SSM_WIDTH ** -0.5),
        "w_out": nrm(ks[14], (DEPTH, D_MIX, D_MODEL), D_MIX ** -0.5),
        "norm_mlp_pre": gain(ks[15], (DEPTH, D_MODEL)),
        "norm_mlp_post": gain(ks[16], (DEPTH, D_MODEL)),
        "w_ff1": nrm(ks[17], (DEPTH, D_MODEL, D_FF), D_MODEL ** -0.5),
        "w_ff2": nrm(ks[18], (DEPTH, D_FF, D_MODEL), D_FF ** -0.5),
    }

def first_block(x, norm_mix_pre, norm_mix_post, w_in, ret_gn_gain, ssm_lambda_re, ssm_lambda_im,
              ssm_log_dt, ssm_b_re, ssm_b_im, ssm_c_re, ssm_c_im, ssm_d, w_glu, w_out,
              norm_mlp_pre, norm_mlp_post, w_ff1, w_ff2):
    B, L, _ = x.shape
    for i in range(DEPTH):
        h = rmsnorm(x, norm_mix_pre[i])
        proj = h @ w_in[i]
        q, k, v, gate, u = jnp.split(proj, [RET_WIDTH, 2 * RET_WIDTH, 3 * RET_WIDTH, 4 * RET_WIDTH], axis=-1)
        heads = lambda t: t.astype(jnp.float32).reshape(B, L, RET_HEADS, RET_HEAD_DIM)
        qh = rope(heads(q))
        kh = rope(heads(k)) * (RET_HEAD_DIM ** -0.5)
        vh = heads(v)
        y_ret = head_groupnorm(retention_chunkwise(qh, kh, vh), ret_gn_gain[i]).reshape(B, L, RET_WIDTH)
        y_ret = (jax.nn.silu(gate.astype(jnp.float32)) * y_ret).astype(x.dtype)

        y_ssm = jax.nn.gelu(s5_scan(u, ssm_lambda_re[i], ssm_lambda_im[i], ssm_log_dt[i], ssm_b_re[i],
                                    ssm_b_im[i], ssm_c_re[i], ssm_c_im[i], ssm_d[i])).astype(x.dtype)
        glu_a, glu_b = jnp.split(y_ssm @ w_glu[i], 2, axis=-1)
        y_ssm = glu_a * jax.nn.sigmoid(glu_b)

        mix = jnp.concatenate([y_ret, y_ssm], axis=-1) @ w_out[i]
        x = x + rmsnorm(mix, norm_mix_post[i])

        h = rmsnorm(x, norm_mlp_pre[i])
        m = jnp.square(jax.nn.relu(h @ w_ff1[i])) @ w_ff2[i]
        x = x + rmsnorm(m, norm_mlp_post[i])
    return x


_first_inputs = first_inputs


def first_inputs(seed=0):
    import zlib

    import numpy as np

    out = dict(_first_inputs(seed))
    spreads = {}
    factors = {'norm_mix_post': 3.736,
     'ret_gn_gain': 4.486,
     'ssm_lambda_re': 8.0,
     'ssm_b_re': 3.431,
     'ssm_b_im': 3.516,
     'ssm_c_re': 3.503,
     'ssm_c_im': 3.47,
     'norm_mlp_pre': 4.293,
     'norm_mlp_post': 4.948}
    for name, (base, spread) in spreads.items():
        noise = np.random.default_rng([zlib.crc32(name.encode()), seed]).standard_normal(out[name].shape)
        drawn = base * np.exp(spread * noise) if base else spread * noise
        out[name] = __import__('jax').numpy.asarray(drawn.astype(out[name].dtype))
    for name, factor in factors.items():
        out[name] = (out[name] * factor).astype(out[name].dtype)
    return out


CTX_LEN = 256
GRID_W = 64
D_SSM = D_MODEL
SSM_HEADDIM = 64
SSM_HEADS = D_SSM // SSM_HEADDIM
SSM_GROUPS_2 = 2
D_STATE = 128
D_CONV = 5
CHUNK = 128
D_POOL = D_MODEL
POOL_WINDOWS = (2, 4, 8, 16)
POOL_GROUP = D_POOL // len(POOL_WINDOWS)
D_MIX_2 = D_SSM + D_POOL
D_XBC = D_SSM + 2 * SSM_GROUPS_2 * D_STATE
D_IN_PROJ = D_SSM + D_XBC + 2 * SSM_HEADS + D_POOL
D_FF_2 = 4 * D_MODEL
EPS = 1e-6
IN_SPLITS = (D_SSM, D_SSM + D_XBC, D_SSM + D_XBC + 2 * SSM_HEADS)


def rmsnorm_2(x, g):
    xf = x.astype(jnp.float32)
    return xf * lax.rsqrt(jnp.mean(xf * xf, axis=-1, keepdims=True) + EPS) * g.astype(jnp.float32)

def modulate(h, shift, scale):
    return h * (1.0 + scale) + shift

def dwconv_centred(u, w, b):
    c = u.shape[-1]
    k = w.shape[0]
    out = lax.conv_general_dilated(
        u, w.astype(jnp.float32)[:, None, :], window_strides=(1,),
        padding=((k // 2, k // 2),), dimension_numbers=('NWC', 'WIO', 'NWC'),
        feature_group_count=c)
    return out + b.astype(jnp.float32)

def box_mean(u, w, axis):
    L = u.shape[axis]
    cs = jnp.cumsum(u, axis=axis)
    cs = jnp.concatenate([jnp.zeros_like(lax.slice_in_dim(cs, 0, 1, axis=axis)), cs], axis=axis)
    t = jnp.arange(L)
    lo = jnp.clip(t - w // 2, 0, L)
    hi = jnp.clip(t + w // 2, 0, L)
    s = jnp.take(cs, hi, axis=axis) - jnp.take(cs, lo, axis=axis)
    cnt = (hi - lo).astype(u.dtype).reshape((L,) + (1,) * (u.ndim - axis - 1))
    return s / cnt

def pool_mixer(u, pool_w, pool_scale, grid):
    b, l, _ = u.shape
    ug = u.reshape(b, l, len(POOL_WINDOWS), POOL_GROUP)
    outs = []
    for gi, w in enumerate(POOL_WINDOWS):
        ui = ug[:, :, gi]
        if grid:
            rows = l // GRID_W
            v = ui.reshape(b, rows, GRID_W, POOL_GROUP)
            m = box_mean(box_mean(v, w, 1), w, 2).reshape(b, l, POOL_GROUP)
        else:
            m = box_mean(ui, w, 1)
        outs.append(m - ui)
    d = jnp.stack(outs, axis=2)
    y = jnp.einsum('blgc,gcd->blgd', d, pool_w.astype(jnp.float32)).reshape(b, l, D_POOL)
    return y * pool_scale.astype(jnp.float32)

def ssd_chunked(xs, dt, a, bm, cm, h0):
    b, l, h, p = xs.shape
    g, n = bm.shape[2], bm.shape[3]
    r = h // g
    nc = l // CHUNK
    xdt = (xs * dt[..., None]).reshape(b, nc, CHUNK, g, r, p)
    acs = jnp.cumsum((dt * a).reshape(b, nc, CHUNK, g, r), axis=2)
    bc = bm.reshape(b, nc, CHUNK, g, n)
    cc = cm.reshape(b, nc, CHUNK, g, n)
    lower = jnp.tril(jnp.ones((CHUNK, CHUNK), dtype=bool))[:, :, None, None]
    seg = acs[:, :, :, None] - acs[:, :, None, :]
    decay = jnp.exp(jnp.where(lower, seg, -jnp.inf))
    cb = jnp.einsum('bctgn,bcsgn->bctsg', cc, bc)
    y_diag = jnp.einsum('bctsgr,bcsgrp->bctgrp', cb[..., None] * decay, xdt)
    st = jnp.einsum('bcsgn,bcsgr,bcsgrp->bcgrpn', bc, jnp.exp(acs[:, :, -1:] - acs), xdt)

    def step(s, inp):
        dec, add = inp
        return s * dec[..., None, None] + add, s

    s_final, s_in = lax.scan(step, h0, (jnp.moveaxis(jnp.exp(acs[:, :, -1]), 1, 0),
                                        jnp.moveaxis(st, 1, 0)))
    s_in = jnp.moveaxis(s_in, 0, 1)
    y_off = jnp.einsum('bctgn,bcgrpn,bctgr->bctgrp', cc, s_in, jnp.exp(acs))
    return (y_diag + y_off).reshape(b, l, h, p), s_final

def ssm_project(h, w_in, conv_w, conv_b, dt_bias):
    b, l, _ = h.shape
    proj = h @ w_in.astype(jnp.float32)
    z, xbc, dt_raw, u = jnp.split(proj, IN_SPLITS, axis=-1)
    xbc = jax.nn.silu(dwconv_centred(xbc, conv_w, conv_b))
    xs, bm, cm = jnp.split(xbc, (D_SSM, D_SSM + SSM_GROUPS_2 * D_STATE), axis=-1)
    xs = xs.reshape(b, l, SSM_HEADS, SSM_HEADDIM)
    bm = bm.reshape(b, l, SSM_GROUPS_2, D_STATE)
    cm = cm.reshape(b, l, SSM_GROUPS_2, D_STATE)
    dt = jax.nn.softplus(dt_raw.reshape(b, l, 2, SSM_HEADS) + dt_bias.astype(jnp.float32))
    return z, xs, bm, cm, dt, u

def bidir_ssd(xs, dt, a_log, bm, cm, h0_f, h0_b):
    a = -jnp.exp(a_log.astype(jnp.float32))
    rev = lambda t: jnp.flip(t, axis=1)
    y_f, s_f = ssd_chunked(xs, dt[:, :, 0], a[0], bm, cm, h0_f)
    y_b, s_b = ssd_chunked(rev(xs), rev(dt[:, :, 1]), a[1], rev(bm), rev(cm), h0_b)
    return y_f + rev(y_b), s_f, s_b

def mixer_out(y_scan, xs, z, u, d_skip, ssm_norm_w, pool_w, pool_scale, w_out, grid):
    b, l = xs.shape[:2]
    y = y_scan + d_skip.astype(jnp.float32)[:, None] * xs
    y = y.reshape(b, l, SSM_GROUPS_2, -1) * jax.nn.silu(z).reshape(b, l, SSM_GROUPS_2, -1)
    y = rmsnorm_2(y, ssm_norm_w.reshape(SSM_GROUPS_2, -1)).reshape(b, l, D_SSM)
    pm = pool_mixer(u, pool_w, pool_scale, grid)
    return jnp.concatenate([y, pm], axis=-1) @ w_out.astype(jnp.float32)

def sq_relu_mlp(h, w1, w2):
    return jnp.square(jax.nn.relu(h @ w1.astype(jnp.float32))) @ w2.astype(jnp.float32)

def second_inputs(seed: int = 0) -> dict:
    key = jax.random.key(seed)
    ks = jax.random.split(key, 24)
    nrm = lambda k, shape, s: jax.random.normal(k, shape, jnp.float32) * s
    dt0 = jnp.exp(jax.random.uniform(ks[13], (DEPTH, 2, SSM_HEADS), jnp.float32,
                                     np.log(1e-3), np.log(1e-1)))
    return {
        "x": nrm(ks[0], (BATCH, SEQ, D_MODEL), 1.0),
        "c": nrm(ks[1], (BATCH, D_MODEL), 1.0),
        "ctx": nrm(ks[2], (BATCH, CTX_LEN, D_MODEL), 1.0),
        "c_ctx": nrm(ks[3], (D_MODEL,), 1.0),
        "w_ada": nrm(ks[4], (DEPTH, D_MODEL, 6 * D_MODEL), 0.5 * D_MODEL ** -0.5),
        "b_ada": nrm(ks[5], (DEPTH, 6 * D_MODEL), 0.02),
        "pre_mix_g": 1.0 + nrm(ks[6], (DEPTH, D_MODEL), 0.02),
        "post_mix_g": 1.0 + nrm(ks[7], (DEPTH, D_MODEL), 0.02),
        "pre_mlp_g": 1.0 + nrm(ks[8], (DEPTH, D_MODEL), 0.02),
        "post_mlp_g": 1.0 + nrm(ks[9], (DEPTH, D_MODEL), 0.02),
        "w_in": nrm(ks[10], (DEPTH, D_MODEL, D_IN_PROJ), D_MODEL ** -0.5),
        "conv_w": nrm(ks[11], (DEPTH, D_CONV, D_XBC), D_CONV ** -0.5),
        "conv_b": nrm(ks[12], (DEPTH, D_XBC), 0.02),
        "dt_bias": dt0 + jnp.log(-jnp.expm1(-dt0)),
        "a_log": jnp.log(jax.random.uniform(ks[14], (DEPTH, 2, SSM_HEADS), jnp.float32, 1.0, 16.0)),
        "d_skip": 1.0 + nrm(ks[15], (DEPTH, SSM_HEADS), 0.1),
        "ssm_norm_w": 1.0 + nrm(ks[16], (DEPTH, D_SSM), 0.02),
        "pool_w": nrm(ks[17], (DEPTH, len(POOL_WINDOWS), POOL_GROUP, POOL_GROUP), POOL_GROUP ** -0.5),
        "pool_scale": 1.0 + nrm(ks[18], (DEPTH, D_POOL), 0.1),
        "w_out": nrm(ks[19], (DEPTH, D_MIX_2, D_MODEL), D_MIX_2 ** -0.5),
        "w_mlp1": nrm(ks[20], (DEPTH, D_MODEL, D_FF_2), D_MODEL ** -0.5),
        "w_mlp2": nrm(ks[21], (DEPTH, D_FF_2, D_MODEL), D_FF_2 ** -0.5),
    }

def second_block(x, c, ctx, c_ctx, w_ada, b_ada, pre_mix_g, post_mix_g, pre_mlp_g, post_mlp_g,
              w_in, conv_w, conv_b, dt_bias, a_log, d_skip, ssm_norm_w, pool_w, pool_scale,
              w_out, w_mlp1, w_mlp2):
    b = x.shape[0]
    xs_ = x.astype(jnp.float32)
    cs_ = ctx.astype(jnp.float32)
    h0 = jnp.zeros((b, SSM_GROUPS_2, SSM_HEADS // SSM_GROUPS_2, SSM_HEADDIM, D_STATE), jnp.float32)
    for i in range(DEPTH):
        wa = w_ada[i].astype(jnp.float32)
        ba = b_ada[i].astype(jnp.float32)
        ada = (jax.nn.silu(c.astype(jnp.float32)) @ wa + ba)[:, None, :]
        sh1, sc1, g1, sh2, sc2, g2 = jnp.split(ada, 6, axis=-1)
        ada_c = jax.nn.silu(c_ctx.astype(jnp.float32)) @ wa + ba
        csh1, csc1, cg1, csh2, csc2, cg2 = jnp.split(ada_c, 6, axis=-1)
        hc = modulate(rmsnorm_2(cs_, pre_mix_g[i]), csh1, csc1)
        zc, xc, bc, cc, dtc, uc = ssm_project(hc, w_in[i], conv_w[i], conv_b[i], dt_bias[i])
        yc, s_f, s_b = bidir_ssd(xc, dtc, a_log[i], bc, cc, h0, h0)
        hx = modulate(rmsnorm_2(xs_, pre_mix_g[i]), sh1, sc1)
        zx, xx, bx, cx, dtx, ux = ssm_project(hx, w_in[i], conv_w[i], conv_b[i], dt_bias[i])
        yx, _, _ = bidir_ssd(xx, dtx, a_log[i], bx, cx, s_f, s_b)
        mix_x = mixer_out(yx, xx, zx, ux, d_skip[i], ssm_norm_w[i], pool_w[i], pool_scale[i],
                          w_out[i], True)
        xs_ = xs_ + g1 * rmsnorm_2(mix_x, post_mix_g[i])
        hm = modulate(rmsnorm_2(xs_, pre_mlp_g[i]), sh2, sc2)
        xs_ = xs_ + g2 * rmsnorm_2(sq_relu_mlp(hm, w_mlp1[i], w_mlp2[i]), post_mlp_g[i])
        if i < DEPTH - 1:
            mix_c = mixer_out(yc, xc, zc, uc, d_skip[i], ssm_norm_w[i], pool_w[i], pool_scale[i],
                              w_out[i], False)
            cs_ = cs_ + cg1 * rmsnorm_2(mix_c, post_mix_g[i])
            hcm = modulate(rmsnorm_2(cs_, pre_mlp_g[i]), csh2, csc2)
            cs_ = cs_ + cg2 * rmsnorm_2(sq_relu_mlp(hcm, w_mlp1[i], w_mlp2[i]), post_mlp_g[i])
    return xs_.astype(x.dtype)


_first_inputs_2 = second_inputs


def second_inputs(seed=0):
    import zlib

    import numpy as np

    out = dict(_first_inputs_2(seed))
    spreads = {}
    factors = {'ctx': 8.0,
     'c_ctx': 8.0,
     'pre_mix_g': 7.458,
     'post_mix_g': 22.856,
     'pre_mlp_g': 31.221,
     'post_mlp_g': 32.311,
     'conv_b': 55.348,
     'd_skip': 64.0,
     'ssm_norm_w': 64.0,
     'pool_scale': 2.775}
    for name, (base, spread) in spreads.items():
        noise = np.random.default_rng([zlib.crc32(name.encode()), seed]).standard_normal(out[name].shape)
        drawn = base * np.exp(spread * noise) if base else spread * noise
        out[name] = __import__('jax').numpy.asarray(drawn.astype(out[name].dtype))
    for name, factor in factors.items():
        out[name] = (out[name] * factor).astype(out[name].dtype)
    return out


_narrow_inputs = second_inputs


def second_inputs(seed=0):

    out = dict(_narrow_inputs(seed))
    wider = {'pre_mlp_g': 3.7, 'post_mlp_g': 3.81, 'd_skip': 12.0, 'ssm_norm_w': 3.25}
    for name, times in wider.items():
        mean = out[name].mean()
        out[name] = (mean + times * (out[name] - mean)).astype(out[name].dtype)
    return out


def setup_inputs(seed=0):
    out = dict(first_inputs(seed))
    for name, value in second_inputs(seed + 1).items():
        if name != "x":
            out[name + "_2"] = value
    return out


def reference(
    x, norm_mix_pre, norm_mix_post, w_in, ret_gn_gain, ssm_lambda_re, ssm_lambda_im, ssm_log_dt,
    ssm_b_re, ssm_b_im, ssm_c_re, ssm_c_im, ssm_d, w_glu, w_out, norm_mlp_pre, norm_mlp_post,
    w_ff1, w_ff2, c_2, ctx_2, c_ctx_2, w_ada_2, b_ada_2, pre_mix_g_2, post_mix_g_2, pre_mlp_g_2,
    post_mlp_g_2, w_in_2, conv_w_2, conv_b_2, dt_bias_2, a_log_2, d_skip_2, ssm_norm_w_2,
    pool_w_2, pool_scale_2, w_out_2, w_mlp1_2, w_mlp2_2,
):
    x = first_block(
        x, norm_mix_pre, norm_mix_post, w_in, ret_gn_gain, ssm_lambda_re, ssm_lambda_im,
        ssm_log_dt, ssm_b_re, ssm_b_im, ssm_c_re, ssm_c_im, ssm_d, w_glu, w_out, norm_mlp_pre,
        norm_mlp_post, w_ff1, w_ff2,
    )
    return second_block(
        x, c_2, ctx_2, c_ctx_2, w_ada_2, b_ada_2, pre_mix_g_2, post_mix_g_2, pre_mlp_g_2,
        post_mlp_g_2, w_in_2, conv_w_2, conv_b_2, dt_bias_2, a_log_2, d_skip_2, ssm_norm_w_2,
        pool_w_2, pool_scale_2, w_out_2, w_mlp1_2, w_mlp2_2,
    )


_drawn_inputs = setup_inputs


def setup_inputs(seed=0):
    import zlib

    import numpy as np

    out = dict(_drawn_inputs(seed))
    spreads = {}
    factors = {}
    for name, (base, spread) in spreads.items():
        noise = np.random.default_rng([zlib.crc32(name.encode()), seed]).standard_normal(out[name].shape)
        drawn = base * np.exp(spread * noise) if base else spread * noise
        out[name] = __import__('jax').numpy.asarray(drawn.astype(out[name].dtype))
    for name, factor in factors.items():
        out[name] = (out[name] * factor).astype(out[name].dtype)
    return out
```

```python
import math
from contextlib import ExitStack

import numpy as np
import concourse.bass as bass
from concourse import mybir
from concourse.alu_op_type import AluOpType as ALU

F32 = mybir.dt.float32
F32R = mybir.dt.float32r
ACT = mybir.ActivationFunctionType

P = 128
D_MODEL = 1024
SEQ = 1024
KT = D_MODEL // P
NC = SEQ // P
HALF = 512
EPS = 1e-6

HEADS = 4
HEAD_DIM = 128
GROUPS = 32
STATE = 64
GROUP_CH = 16
STEP = P // GROUP_CH
NBLK = SEQ // STEP
FT = 4
GPT = GROUPS // FT
GT = GPT // 2
D_FF = 4096
HID = 4
MLP_STEPS = D_FF // P // HID

CTX = 256
CC = CTX // P
TOK2 = CTX + SEQ
SSM_HEADS = 16
HDIM = 64
NGRP = 2
HPG = SSM_HEADS // NGRP
XBC_TILES = 12
TAPS = 5
GRID_W = 64
ROWS = SEQ // GRID_W
WINDOWS = (2, 4, 8, 16)

TWO_PI = 2.0 * math.pi
ROUND = 12582912.0
PI2_A = 6.28125
PI2_B = float((np.float32(TWO_PI - 6.28125).view(np.uint32) & np.uint32(0xFFFFF000)).view(np.float32))
PI2_C = TWO_PI - PI2_A - PI2_B
PI_LOW = 3.1415925

VEC = {}
_at = 0
for _name, _n in (("mix_pre", KT), ("mix_post", KT), ("mlp_pre", KT), ("mlp_post", KT), ("gn", HEADS),
                  ("mix_pre2", KT), ("mix_post2", KT), ("mlp_pre2", KT), ("mlp_post2", KT),
                  ("ssm_norm", KT), ("pool_scale", KT), ("conv_w", XBC_TILES * TAPS),
                  ("conv_b", XBC_TILES), ("b_ada", 48), ("c", 2 * KT)):
    VEC[_name] = (_at, _at + _n)
    _at += _n
VEC_COLS = _at

PRM = {}
_at = 0
for _name, _n in (("lre", GT), ("lim", GT), ("ldt", GT), ("bre", GT * GROUP_CH), ("bim", GT * GROUP_CH),
                  ("cre", GT * GROUP_CH), ("cim", GT * GROUP_CH)):
    PRM[_name] = (_at, _at + _n)
    _at += _n
PRM_COLS = _at

HC_DECAY, HC_XI, HC_ZETA, HC_GAMMA = 0, P, 2 * P, 2 * P + 1
HC_COLS = 2 * P + 2

IDENT, CENTER, TRI_LE, TRI_GE, TRI_GT, TRI_LT = range(6)

STEP_LINKS = 328

P1_TILES = HEADS * 5
GLU_TILES = 4
P2_TILES = GLU_TILES + KT
MLP_TILES = MLP_STEPS * 2 * HID
XBC_END = P1_TILES + P2_TILES + MLP_TILES + XBC_TILES
UZ_END = XBC_END + 2 * KT
OUT2_END = UZ_END + 2 + 2 * KT
ALL_TILES = OUT2_END + MLP_TILES


class Chain:

    def __init__(self, eng, sem):
        self.eng, self.sem, self.base, self.n = eng, sem, 0, 0

    def link(self, ins):
        self.n += 1
        ins.then_inc(self.sem, 1)
        self.eng.wait_ge(self.sem, self.base + self.n)

    def mark(self, ins):
        self.n += 1
        ins.then_inc(self.sem, 1)

    def enter(self, i, per):
        self.start = self.base
        self.base, self.n, self.per, self.outer = self.start + self.n + i * per, 0, per, self.start + self.n

    def leave(self, count):
        assert self.n == self.per, f"{self.n} links in the loop's body, not {self.per}"
        self.base, self.n = self.outer + count * self.per, 0


def bc(ap, dim, n):
    ap = ap.unsqueeze(dim)
    shape = list(ap.shape)
    shape[dim] = n
    return ap.broadcast_to(shape)


class Kit:
    pass


def open_kit(nc, ctx, d):
    k = Kit()

    def sb(name, shape, dt=F32):
        return ctx.enter_context(nc.sbuf_tensor(name, shape, dt))

    def sem(name):
        return ctx.enter_context(nc.semaphore(name))

    k.wstream = d.wstream
    k.ps = ctx.enter_context(nc.psum_tensor("ps", [P, 8, HALF], F32))
    k.w_raw = sb("w_raw", [P, 2, KT * P])
    k.w_hi, k.w_lo = sb("w_hi", [P, 2, KT * P], F32R), sb("w_lo", [P, 2, KT * P], F32R)
    k.mats = sb("mats", [P, 6, P])
    k.vecs = sb("vecs", [P, VEC_COLS])
    k.zeros = sb("zeros", [P, 1])
    k.mean_col, k.head_col, k.eps = sb("mean_col", [P, 1]), sb("head_col", [P, 1]), sb("eps", [P, 1])
    k.c_silu = sb("c_silu", [P, KT, 2])
    k.ada_w = sb("ada_w", [P, KT * P])
    k.ada = sb("ada", [P, 48, 2])
    k.mod = sb("mod", [P, 8, KT])
    k.w_loaded = [sem("w_loaded0"), sem("w_loaded1")]
    k.w_high, k.w_split, k.tile_done, k.zeroed = sem("w_high"), sem("w_split"), sem("tile_done"), sem("zeroed")
    k.pair_free = [sem("pair_free0"), sem("pair_free1")]
    k.aux_done = sem("aux_done")
    k.aux_free = [sem("aux_free0"), sem("aux_free1")]
    return k


def stream_load(sp, k, first, last):
    with sp.Fori(0, (last - first) // 2) as j:
        for s in range(2):
            n = first + 2 * j + s
            if first:
                sp.wait_ge(k.w_split, n - 1)
            else:
                sp.wait_ge(k.w_split, 2 * j)
            sp.dma_start(k.w_raw[:, s, :], k.wstream[bass.ds(n, 1), :, :].rearrange("a p c -> p (a c)"))\
              .then_inc(k.w_loaded[s], 16)


def stream_split(pool, k, first, last):
    with pool.Fori(0, (last - first) // 2) as j:
        for s in range(2):
            n = first + 2 * j + s
            pool.wait_ge(k.w_loaded[s], (j + first // 2 + 1) * 16)
            if first:
                pool.wait_ge(k.tile_done, n - 1)
            else:
                pool.wait_ge(k.tile_done, 2 * j)
            pool.tensor_tensor(k.w_hi[:, s, :], k.w_raw[:, s, :], k.zeros[:, 0:1].broadcast_to([P, KT * P]),
                               ALU.add).then_inc(k.w_high, 1)
            pool.wait_ge(k.w_high, n + 1)
            pool.tensor_tensor(k.w_lo[:, s, :], k.w_raw[:, s, :], k.w_hi[:, s, :].bitcast(F32),
                               ALU.subtract).then_inc(k.w_split, 1)


def products(pe, w_hi, w_lo, a_hi, a_lo, outs, first, last):
    for o, c in outs:
        pe.matmul(o, w_hi, a_hi[:, c], start=first, stop=False)
    for o, c in outs:
        pe.matmul(o, w_hi, a_lo[:, c], start=False, stop=False)
    for o, c in outs:
        ins = pe.matmul(o, w_lo, a_hi[:, c], start=False, stop=last)
    return ins


def tile_products(pe, k, s, hi, lo, outs, kts=KT, at=0, kt0=0):
    for kt in range(kts):
        c = slice(at + kt * P, at + (kt + 1) * P)
        ins = products(pe, k.w_hi[:, s, c], k.w_lo[:, s, c], hi[:, kt0 + kt, :], lo[:, kt0 + kt, :], outs,
                       kt == 0, kt == kts - 1)
    return ins


def both_halves(k, s):
    return [(k.ps[:, 2 * s + h, :], slice(h * HALF, (h + 1) * HALF)) for h in range(2)]


def gemm(pe, k, n, s, uses, hi, lo, outs=None):
    pe.wait_ge(k.w_split, n + 1)
    pe.wait_ge(k.pair_free[s], uses)
    tile_products(pe, k, s, hi, lo, outs or both_halves(k, s)).then_inc(k.tile_done, 1)


def ada_products(pe, k, out):
    for kt in range(KT):
        ins = pe.matmul(out[:, 0:2], k.ada_w[:, kt * P:(kt + 1) * P], k.c_silu[:, kt, :],
                        start=kt == 0, stop=kt == KT - 1)
    return ins


def phase1(nc, k, d):
    with ExitStack() as ctx:
        def sb(name, shape, dt=F32):
            return ctx.enter_context(nc.sbuf_tensor(name, shape, dt))

        def sem(name):
            return ctx.enter_context(nc.semaphore(name))

        h_hi, h_lo = sb("h1_hi", [P, KT, SEQ], F32R), sb("h1_lo", [P, KT, SEQ], F32R)
        cosr, sinr, rstd = sb("cosr", [P, SEQ]), sb("sinr", [P, SEQ]), sb("rstd1", [P, SEQ])
        raw, swap = sb("raw", [P, SEQ]), sb("swap", [P, SEQ])
        kT, qT, vT, uT, qxi = (sb(n, [P, SEQ]) for n in ("kT", "qT", "vT", "uT", "qxi"))
        u_blk, u_grp = sb("u_blk", [P, SEQ]), sb("u_grp", [P, GPT, NBLK])
        k_tok, v_tok, sT, R = (sb(n, [P, NC, P]) for n in ("k_tok", "v_tok", "sT", "R"))
        yc = sb("yc", [P, SEQ])
        hT, mT = sb("hT", [P, 2, GT, P]), sb("mT", [P, GPT, P])
        hs = sb("hs", [P, 2, GT, STEP, GROUP_CH])
        gg = sb("gg", [P, 2, GT, STEP + 1, GROUP_CH])
        t1, t2 = (sb(n, [P, GT * (STEP + 1) * GROUP_CH]) for n in ("t1", "t2"))
        rot, z, xp = (sb(n, [P, 2, GT, NBLK]) for n in ("rot", "z", "xp"))
        decay8 = sb("decay8", [P, GT, NBLK])
        k_rows = z[0:GROUP_CH, :, :, :].rearrange("p a g n -> p (a g) n")
        prm, hc = sb("prm", [P, PRM_COLS]), sb("hc", [P, HC_COLS])
        ang, kk, sn, cs = (sb(n, [P, 8, GT]) for n in ("ang", "kk", "sn", "cs"))
        pw, sm = sb("pw", [P, 2, STEP + 1, GT]), sb("sm", [P, 12, GT])
        bb = sb("bb", [P, 2, GT, GROUP_CH])
        dm = sb("dm", [GROUP_CH, GROUPS])
        col, rcol = sb("col1", [P, NC]), sb("rcol1", [P, NC])

        x_in = [sem("x_in0"), sem("x_in1")]
        (x_sq, x_sum, xg_made, h_high, h_split, const_in, ones_set, silu_done, sums_done, root_done,
         inv_done, rstd_row, rope_scaled, dve_chain, act_chain) = (sem(n) for n in (
             "x_sq", "x_sum", "xg_made", "h_high", "h_split", "const_in", "ones_set", "silu_done", "sums_done", "root_done", "inv_done", "rstd_row", "rope_scaled", "dve1_chain", "act1_chain"))
        (prm_in, head_in, ada_in, dt_ready, mag_ready, exps_ready, ang_ready, sin_ready, hs_ready, gg_ready, rows_ready, mT_in,
         raw_ready, swap_ready, kT_ready, qT_ready, qxi_ready, xp_ready, y_half, rows_begin, gate_ready, sq_ready, inv_ready,
         ret_ready, ssm_out, ret_out) = (sem(n) for n in (
             "prm_in", "head_in", "ada_in", "dt_ready", "mag_ready", "exps_ready", "ang_ready", "sin_ready", "hs_ready",
             "gg_ready", "rows_ready", "mT_in", "raw_ready", "swap_ready", "kT_ready", "qT_ready", "qxi_ready",
             "xp_ready", "y_half", "rows_begin", "gate_ready", "sq_ready", "inv_ready", "ret_ready", "ssm_out", "ret_out"))

        tiles = 5
        U_, K_, V_, Q_, G_ = range(tiles)
        J = 20
        (ADA0, ADA1, HT_RE, HT_IM, K_ROWS, ADA2, ADA3, U_BLOCKS, U_GROUPS, STATES, K_TOK, V_TOK, KV, SSM_Y, SCORES, SSM_T, RET_Y, CENTRED,
         VARIANCE, RSTD) = range(J)
        X = [k.ps[:, 4:6, :], k.ps[:, 6:8, :]]
        Xf = [x.rearrange("p a b -> p (a b)") for x in X]
        pair = [k.ps[:, 2 * s:2 * s + 2, :].rearrange("p a b -> p (a b)") for s in range(2)]
        ident = k.mats[:, IDENT, :]

        def slot(half, t):
            return (half * tiles + t) % 2

        def uses(jj, half, t):
            return jj * tiles + (half * tiles + t) // 2

        def auxes(i, j):
            return i * (J // 2) + j // 2

        block = ctx.enter_context(nc.Block())

        @block.sync
        def _(sp):
            sp.dma_start(k.mats[:, :, :], d.mats.rearrange("m p c -> p m c")).then_inc(const_in, 16)
            sp.dma_start(k.vecs[:, :], d.vecs).then_inc(const_in, 16)
            for t in range(KT):
                if t >= 2:
                    sp.wait_ge(x_sq, t - 1)
                    sp.wait_ge(xg_made, t - 1)
                sp.dma_start((raw, swap)[t % 2][:, :], d.xT[:, t, :]).then_inc(x_in[t % 2], 16)
            sp.dma_start(dm[:, :], d.d_rows).then_inc(const_in, 16)
            sp.dma_start(cosr[:, :], d.rope[0, :, :]).then_inc(const_in, 16)
            sp.dma_start(sinr[:, :], d.rope[1, :, :]).then_inc(const_in, 16)
            stream_load(sp, k, 0, P1_TILES + 4)

        @block.gpsimd
        def _(pool):
            pool.memset(k.zeros[:, :], 0.0).then_inc(k.zeroed, 1)
            pool.wait_ge(k.zeroed, 1)
            stream_split(pool, k, 0, P1_TILES + 2)

        @block.tensor
        def _(pe):
            pe.wait_ge(x_sum, KT)
            pe.wait_ge(ones_set, 2)
            pe.wait_ge(const_in, 80)
            for c in range(NC):
                ins = pe.matmul(Xf[0][:, c:c + 1], yc[:, c * P:(c + 1) * P], k.mean_col[:, :], start=True, stop=True)
            ins.then_inc(sums_done, 1)
            pe.wait_ge(inv_done, 1)
            for c in range(NC):
                ins = pe.matmul(Xf[1][:, c * P:(c + 1) * P], rcol[:, c:c + 1].broadcast_to([P, P]), ident,
                                start=True, stop=True)
            ins.then_inc(rstd_row, 1)
            pe.wait_ge(h_split, KT)
            pe.wait_ge(silu_done, 1)
            pe.wait_ge(rope_scaled, 3)
            def step(jj, half):
                i = 2 * jj + half

                def tile(t):
                    gemm(pe, k, i * tiles + t, slot(half, t), uses(jj, half, t), h_hi, h_lo)

                def ada(j, a):
                    job(j)
                    pe.wait_ge(ada_in, (4 * i + a + 1) * 16)
                    ada_products(pe, k, X[j % 2][:, 0, :]).then_inc(k.aux_done, 1)

                def job(j):
                    pe.wait_ge(k.aux_free[j % 2], auxes(i, j))

                def read(j):
                    pe.wait_ge(k.aux_free[j % 2], auxes(i, j) + 1)

                def transposes(j, sources):
                    for c, src in enumerate(sources):
                        ins = pe.transpose(Xf[j % 2][:, c * P:(c + 1) * P], src, ident)
                    ins.then_inc(k.aux_done, 1)

                ada(ADA0, 0)
                tile(U_)
                ada(ADA1, 1)
                for j in (HT_RE, HT_IM):
                    job(j)
                    pe.wait_ge(hs_ready, i + 1)
                    transposes(j, [hs[:, j % 2, g, :, :].rearrange("p t c -> p (t c)") for g in range(GT)])
                job(K_ROWS)
                pe.wait_ge(gg_ready, i + 1)
                pe.sem_inc(rows_begin, 1)
                for g in range(GPT):
                    q = slice(64 * (g % 2), 64 * (g % 2) + 64)
                    for r in range(2):
                        ins = pe.matmul(X[0][0:GROUP_CH, g % 2, (g // 2) * P:(g // 2 + 1) * P], bb[q, r, g // 2, :],
                                        gg[q, r, g // 2, 0:STEP, :].rearrange("p t c -> p (t c)"),
                                        start=r == 0, stop=r == 1)
                ins.then_inc(k.aux_done, 1)
                ada(ADA2, 2)
                tile(K_)
                ada(ADA3, 3)
                job(U_BLOCKS)
                pe.wait_ge(k.pair_free[slot(half, U_)], uses(jj, half, U_) + 1)
                transposes(U_BLOCKS, [uT[:, :].rearrange("p (n t) -> p t n", t=STEP)[:, t, :] for t in range(STEP)])
                job(U_GROUPS)
                read(U_BLOCKS)
                transposes(U_GROUPS, [u_blk[:, g * P:(g + 1) * P] for g in range(GPT)])
                tile(V_)
                job(STATES)
                read(U_GROUPS)
                read(HT_IM)
                for r in range(2):
                    for g in range(GPT):
                        q = slice(64 * (g % 2), 64 * (g % 2) + 64)
                        ins = pe.matmul(X[1][q, r, (g // 2) * P:(g // 2 + 1) * P], hT[:, r, g // 2, q],
                                        u_grp[:, g, :], start=True, stop=True)
                ins.then_inc(k.aux_done, 1)
                tile(Q_)
                job(K_TOK)
                pe.wait_ge(kT_ready, i + 1)
                transposes(K_TOK, [kT[:, c * P:(c + 1) * P] for c in range(NC)])
                tile(G_)
                job(V_TOK)
                pe.wait_ge(k.pair_free[slot(half, V_)], uses(jj, half, V_) + 1)
                transposes(V_TOK, [vT[:, c * P:(c + 1) * P] for c in range(NC)])
                job(KV)
                read(K_TOK)
                read(V_TOK)
                for c in range(NC - 1):
                    ins = pe.matmul(Xf[0][:, c * P:(c + 1) * P], k_tok[:, c, :], v_tok[:, c, :], start=True, stop=True)
                ins.then_inc(k.aux_done, 1)
                job(SSM_Y)
                pe.wait_ge(xp_ready, i + 1)
                pe.wait_ge(mT_in, (i + 1) * (16 * STEP))
                for g in range(GPT):
                    q = slice(64 * (g % 2), 64 * (g % 2) + 64)
                    o = X[1][:, g % 2, (g // 2) * P:(g // 2 + 1) * P]
                    pe.matmul(o, u_grp[:, g, :], mT[:, g, :], start=True, stop=False)
                    for r in range(2):
                        ins = pe.matmul(o, xp[q, r, g // 2, :],
                                        gg[q, r, g // 2, 1:STEP + 1, :].rearrange("p t c -> p (t c)"),
                                        start=False, stop=r == 1)
                ins.then_inc(k.aux_done, 1)
                job(SCORES)
                pe.wait_ge(qT_ready, i + 1)
                for c in range(NC):
                    s = slice(c * P, (c + 1) * P)
                    ins = pe.matmul(Xf[0][:, s], kT[:, s], qT[:, s], start=True, stop=True)
                ins.then_inc(k.aux_done, 1)
                job(SSM_T)
                read(SSM_Y)
                transposes(SSM_T, [u_blk[:, t * P:(t + 1) * P] for t in range(STEP)])
                job(RET_Y)
                read(SCORES)
                read(KV)
                pe.wait_ge(qxi_ready, i + 1)
                for c in range(NC):
                    s = slice(c * P, (c + 1) * P)
                    ins = pe.matmul(Xf[0][:, s], v_tok[:, c, :], sT[:, c, :], start=True, stop=c == 0)
                    if c:
                        ins = pe.matmul(Xf[0][:, s], R[:, c, :], qxi[:, s], start=False, stop=True)
                ins.then_inc(k.aux_done, 1)
                job(CENTRED)
                read(RET_Y)
                for h in range(2):
                    ins = pe.matmul(X[1][:, h, :], k.mats[:, CENTER, :], raw[:, h * HALF:(h + 1) * HALF],
                                    start=True, stop=True)
                ins.then_inc(k.aux_done, 1)
                job(VARIANCE)
                pe.wait_ge(sq_ready, i + 1)
                for c in range(NC):
                    ins = pe.matmul(Xf[0][:, c:c + 1], swap[:, c * P:(c + 1) * P], k.head_col[:, :], start=True, stop=True)
                ins.then_inc(k.aux_done, 1)
                job(RSTD)
                pe.wait_ge(inv_ready, i + 1)
                for c in range(NC):
                    ins = pe.matmul(Xf[1][:, c * P:(c + 1) * P], rcol[:, c:c + 1].broadcast_to([P, P]), ident,
                                    start=True, stop=True)
                ins.then_inc(k.aux_done, 1)

            with pe.Fori(0, HEADS // 2) as jj:
                step(jj, 0)
                step(jj, 1)

        @block.scalar
        def _(act):
            act.dma_start(prm[:, :], d.prm[0, :, :]).then_inc(prm_in, 16)
            act.dma_start(hc[:, :], d.head_consts[0, :, :]).then_inc(head_in, 16)
            act.dma_start(k.ada_w[:, :], d.ada_w[0, :, :]).then_inc(ada_in, 16)
            act.wait_ge(const_in, 32)
            for t in range(KT):
                act.wait_ge(x_in[t % 2], 16 * (t // 2 + 1))
                if t > 1:
                    act.wait_ge(x_sum, t)
                (act.activation((kT, qT)[t % 2][:, :] if t else yc[:, :], (raw, swap)[t % 2][:, :], ACT.Square)
                 .then_inc(x_sq, 1))
                act.wait_ge(xg_made, t + 1)
                act.activation(h_hi[:, t, :], (vT, uT)[t % 2][:, :], ACT.Copy).then_inc(h_high, 1)
            act.wait_ge(sums_done, 1)
            act.wait_ge(ones_set, 2)
            act.activation(col[:, :], Xf[0][:, 0:NC], ACT.Sqrt, bias=k.eps[:, :]).then_inc(root_done, 1)
            a, b = VEC["c"]
            act.activation(k.c_silu[:, :, :].rearrange("p a b -> p (a b)"), k.vecs[:, a:b], ACT.Silu)\
               .then_inc(silu_done, 1)

            def step(jj, half):
                i = 2 * jj + half

                def ada(j, a):
                    job(j)
                    act.activation(k.ada[:, bass.ds(4 * i + a, 1), :].rearrange("p a c -> p (a c)"),
                                   X[j % 2][:, 0, 0:2], ACT.Copy).then_inc(k.aux_free[j % 2], 1)
                    act.dma_start(k.ada_w[:, :], d.ada_w[bass.ds(4 * i + a + 1, 1), :, :]
                                  .rearrange("a p c -> p (a c)")).then_inc(ada_in, 16)

                def job(j):
                    act.wait_ge(k.aux_done, i * J + j + 1)

                def halves_swapped(t, when):
                    s = slot(half, t)
                    act.wait_ge(k.tile_done, i * tiles + t + 1)
                    act.activation(raw[:, :], pair[s], ACT.Copy).then_inc(raw_ready, 1)
                    act.activation(swap[0:64, :], pair[s][64:128, :], ACT.Copy).then_inc(swap_ready, 1)
                    act.wait_ge(raw_ready, 2 * i + when)
                    act.wait_ge(swap_ready, 2 * i + when)
                    act.activation(swap[64:128, :], pair[s][0:64, :], ACT.Copy).then_inc(k.pair_free[s], 1)

                ada(ADA0, 0)
                act.wait_ge(prm_in, 16 * (i + 1))
                act.activation(sm[:, 0, :], prm[:, PRM["ldt"][0]:PRM["ldt"][1]], ACT.Exp).then_inc(dt_ready, 1)
                act.wait_ge(mag_ready, i + 1)
                act.activation(sm[:, 3, :], sm[:, 2, :], ACT.Exp).then_inc(exps_ready, 1)
                act.activation(sm[:, 4, :], sm[:, 2, :], ACT.Exp, scale=float(STEP)).then_inc(exps_ready, 1)
                act.wait_ge(ang_ready, i + 1)
                act.activation(sn[:, :, :], ang[:, :, :], ACT.Sin).then_inc(sin_ready, 1)
                act.activation(cs[:, :, :], ang[:, :, :], ACT.Sin, scale=0.5).then_inc(sin_ready, 1)
                ada(ADA1, 1)
                for j in (HT_RE, HT_IM):
                    job(j)
                    act.activation(hT[:, j % 2, :, :].rearrange("p g s -> p (g s)"), X[j % 2][:, 0, :], ACT.Copy)\
                       .then_inc(k.aux_free[j % 2], 1)
                ada(ADA2, 2)
                act.wait_ge(rows_ready, i + 1)
                for t in range(STEP):
                    act.dma_start(mT[GROUP_CH * t:GROUP_CH * (t + 1), :, GROUP_CH * t:P],
                                  k_rows[:, :, 0:P - GROUP_CH * t]).then_inc(mT_in, 16)
                act.dma_start(prm[:, :], d.prm[bass.ds(i + 1, 1), :, :].rearrange("a p c -> p (a c)"))\
                   .then_inc(prm_in, 16)
                halves_swapped(K_, 1)
                ada(ADA3, 3)
                job(U_BLOCKS)
                act.activation(u_blk[:, :].rearrange("p (g t c) -> p t g c", g=GPT, c=GROUP_CH),
                               Xf[1].rearrange("p (t g c) -> p t g c", g=GPT, c=GROUP_CH), ACT.Copy)\
                   .then_inc(k.aux_free[1], 1)
                job(U_GROUPS)
                act.activation(u_grp[:, :, :].rearrange("p g n -> p (g n)"), Xf[0], ACT.Copy).then_inc(k.aux_free[0], 1)
                act.wait_ge(kT_ready, i + 1)
                halves_swapped(Q_, 2)
                act.wait_ge(head_in, 16 * (i + 1))
                job(K_TOK)
                act.activation(k_tok[:, :, :].rearrange("p c j -> p (c j)"), Xf[0], ACT.Copy,
                               scale=hc[:, HC_ZETA:HC_ZETA + 1]).then_inc(k.aux_free[0], 1)
                job(V_TOK)
                act.activation(v_tok[:, :, :].rearrange("p c j -> p (c j)"), Xf[1], ACT.Copy).then_inc(k.aux_free[1], 1)
                act.wait_ge(k.pair_free[slot(half, G_)], uses(jj, half, G_) + 1)
                act.activation(vT[:, :], vT[:, :], ACT.Silu).then_inc(gate_ready, 1)
                job(SSM_Y)
                for h in range(2):
                    act.activation(u_blk[:, :].rearrange("p (t g c) -> p g t c", g=GPT, c=GROUP_CH)[:, h:GPT:2, :, :],
                                   X[1][:, h, :].rearrange("p (g t c) -> p g t c", t=STEP, c=GROUP_CH),
                                   ACT.Gelu_apprx_tanh).then_inc((y_half, k.aux_free[1])[h], 1)
                    if h == 0:
                        act.wait_ge(y_half, i + 1)
                job(SSM_T)
                act.activation(uT[:, :].rearrange("p (n t) -> p t n", t=STEP),
                               Xf[1].rearrange("p (t n) -> p t n", n=NBLK), ACT.Copy).then_inc(k.aux_free[1], 1)
                act.wait_ge(k.aux_free[1], auxes(i, SSM_T) + 1)
                act.dma_start(d.y_scr[bass.ds(i + HEADS, 1), :, :].rearrange("a p c -> p (a c)"), uT[:, :])\
                   .then_inc(ssm_out, 16)
                job(RET_Y)
                act.wait_ge(qT_ready, i + 1)
                act.activation(raw[:, :], Xf[0], ACT.Copy).then_inc(k.aux_free[0], 1)
                job(CENTRED)
                act.activation(swap[:, :], Xf[1], ACT.Square).then_inc(sq_ready, 1)
                act.wait_ge(ret_out, 16 * i)
                act.wait_ge(sq_ready, i + 1)
                act.activation(yc[:, :], Xf[1], ACT.Copy).then_inc(k.aux_free[1], 1)
                job(VARIANCE)
                act.activation(col[:, :], Xf[0][:, 0:NC], ACT.Sqrt, bias=k.eps[:, :]).then_inc(k.aux_free[0], 1)
                act.wait_ge(ret_ready, i + 1)
                act.dma_start(d.y_scr[bass.ds(i, 1), :, :].rearrange("a p c -> p (a c)"), yc[:, :]).then_inc(ret_out, 16)
                act.dma_start(hc[:, :], d.head_consts[bass.ds(i + 1, 1), :, :].rearrange("a p c -> p (a c)"))\
                   .then_inc(head_in, 16)

            with act.Fori(0, HEADS // 2) as jj:
                step(jj, 0)
                step(jj, 1)
            act.wait_ge(ssm_out, 16 * HEADS)
            act.wait_ge(ret_out, 16 * HEADS)
            act.wait_ge(head_in, 16 * (HEADS + 1))
            act.wait_ge(prm_in, 16 * (HEADS + 1))
            act.wait_ge(ada_in, 16 * (4 * HEADS + 1))

        @block.vector
        def _(dve):
            ch = Chain(dve, dve_chain)
            tt, ts, stt = dve.tensor_tensor, dve.tensor_scalar, dve.scalar_tensor_tensor
            dve.memset(k.mean_col[:, :], 1.0 / D_MODEL).then_inc(ones_set, 1)
            dve.wait_ge(ones_set, 1)
            ch.link(dve.memset(k.head_col[:, :], 1.0 / HEAD_DIM))
            dve.memset(k.eps[:, :], EPS).then_inc(ones_set, 1)
            for buf in (pw[:, 1, 0, :], rot[:, 1, :, 0], decay8[:, :, 0], xp[:, :, :, 0], mT[:, :, :]):
                ch.mark(dve.memset(buf, 0.0))
            ch.mark(dve.memset(pw[:, 0, 0, :], 1.0))
            ch.link(dve.memset(rot[:, 0, :, 0], 1.0))
            dve.wait_ge(const_in, 32)
            for t in range(KT):
                dve.wait_ge(x_in[t % 2], 16 * (t // 2 + 1))
                if t >= 2:
                    dve.wait_ge(h_high, t - 1)
                xg = (vT, uT)[t % 2]
                g = VEC["mix_pre"][0] + t
                ts(xg[:, :], (raw, swap)[t % 2][:, :], k.vecs[:, g:g + 1], None, ALU.mult).then_inc(xg_made, 1)
                dve.wait_ge(x_sq, t + 1)
                if t:
                    tt(yc[:, :], yc[:, :], (kT, qT)[t % 2][:, :], ALU.add).then_inc(x_sum, 1)
                else:
                    dve.sem_inc(x_sum, 1)
                dve.wait_ge(h_high, t + 1)
                dve.wait_ge(x_sum, t + 1)
                tt(h_lo[:, t, :], xg[:, :], h_hi[:, t, :].bitcast(F32), ALU.subtract).then_inc(h_split, 1)
            dve.wait_ge(h_split, KT)
            dve.wait_ge(root_done, 1)
            dve.reciprocal(rcol[:, :], col[:, :]).then_inc(inv_done, 1)
            dve.wait_ge(rstd_row, 1)
            dve.wait_ge(const_in, 80)
            dve.tensor_copy(rstd[:, :], Xf[1]).then_inc(rope_scaled, 1)
            dve.wait_ge(rope_scaled, 1)
            tt(cosr[:, :], cosr[:, :], rstd[:, :], ALU.mult).then_inc(rope_scaled, 1)
            tt(sinr[:, :], sinr[:, :], rstd[:, :], ALU.mult).then_inc(rope_scaled, 1)
            dve.wait_ge(rope_scaled, 3)

            def product(out, a, b, n, shape, conj=False):
                x, y = t1[:, 0:n], t2[:, 0:n]
                if len(shape) > 1:
                    names = "abc"[:len(shape)]
                    kw = {c: v for c, v in zip(names[1:], shape[1:])}
                    form = f"p ({' '.join(names)}) -> p {' '.join(names)}"
                    x, y = x.rearrange(form, **kw), y.rearrange(form, **kw)
                ch.mark(tt(x, a[0], b[0], ALU.mult))
                ch.link(tt(y, a[1], b[1], ALU.mult))
                ch.link(tt(out[0], x, y, ALU.add if conj else ALU.subtract))
                ch.mark(tt(x, a[1], b[0], ALU.mult))
                ch.link(tt(y, a[0], b[1], ALU.mult))
                return tt(out[1], x, y, ALU.subtract if conj else ALU.add)

            def step(jj, half):
                i = 2 * jj + half

                def prm_of(name, cols=None):
                    ap = prm[:, PRM[name][0]:PRM[name][1]]
                    return ap if cols is None else ap.rearrange("p (g c) -> p g c", c=cols)

                def job(j):
                    dve.wait_ge(k.aux_done, i * J + j + 1)

                def small(j):
                    return sm[:, j, :]

                dt, lr, a, m1, m8, num, den, fr, fi, s1, s2 = (small(j) for j in (0, 1, 2, 3, 4, 5, 6, 7, 8, 9, 10))
                dve.wait_ge(prm_in, 16 * (i + 1))
                ch.link(ts(lr, prm_of("lre"), -1e-4, None, ALU.min))
                dve.wait_ge(dt_ready, i + 1)
                tt(a, lr, dt, ALU.mult).then_inc(mag_ready, 1)
                ch.link(tt(ang[:, 0, :], prm_of("lim"), dt, ALU.mult))
                for j in range(7):
                    ch.link(ts(ang[:, j + 1, :], ang[:, 0, :], float(STEP << j), None, ALU.mult))
                ch.link(ts(kk[:, :, :], ang[:, :, :], 1.0 / TWO_PI, ROUND, ALU.mult, ALU.add))
                ch.link(ts(kk[:, :, :], kk[:, :, :], ROUND, None, ALU.subtract))
                for part in (PI2_A, PI2_B, PI2_C):
                    ch.link(stt(out=ang[:, :, :], in0=kk[:, :, :], scalar=-part, in1=ang[:, :, :],
                                op0=ALU.mult, op1=ALU.add))
                ts(ang[:, :, :], ang[:, :, :], PI_LOW, -PI_LOW, ALU.min, ALU.max).then_inc(ang_ready, 1)
                dve.wait_ge(sin_ready, 2 * i + 2)
                dve.wait_ge(exps_ready, 2 * i + 2)
                ch.link(tt(cs[:, :, :], cs[:, :, :], cs[:, :, :], ALU.mult))
                ch.link(ts(cs[:, :, :], cs[:, :, :], -2.0, 1.0, ALU.mult, ALU.add))
                ch.mark(tt(pw[:, 0, 1, :], m1, cs[:, 0, :], ALU.mult))
                ch.link(tt(pw[:, 1, 1, :], m1, sn[:, 0, :], ALU.mult))
                for lo, n in ((1, 1), (2, 2), (4, 4)):
                    part = [pw[:, r, 1:1 + n, :] for r in range(2)]
                    base = [bc(pw[:, r, lo, :], 1, n) for r in range(2)]
                    ch.link(product([pw[:, r, lo + 1:lo + 1 + n, :] for r in range(2)], part, base, n * GT, (n, GT)))
                li = prm_of("lim")
                ch.mark(ts(num, pw[:, 0, 1, :], 1.0, None, ALU.subtract))
                ch.mark(tt(s1, lr, lr, ALU.mult))
                ch.link(tt(s2, li, li, ALU.mult))
                ch.link(tt(den, s1, s2, ALU.add))
                ch.link(dve.reciprocal(den, den))
                ch.mark(tt(s1, num, lr, ALU.mult))
                ch.link(tt(s2, pw[:, 1, 1, :], li, ALU.mult))
                ch.link(tt(fr, s1, s2, ALU.add))
                ch.mark(tt(s1, pw[:, 1, 1, :], lr, ALU.mult))
                ch.link(tt(s2, num, li, ALU.mult))
                ch.link(tt(fi, s1, s2, ALU.subtract))
                ch.mark(tt(fr, fr, den, ALU.mult))
                ch.link(tt(fi, fi, den, ALU.mult))
                n = GT * GROUP_CH
                ch.link(product([bb[:, r, :, :] for r in range(2)], [bc(fr, 2, GROUP_CH), bc(fi, 2, GROUP_CH)],
                                [prm_of("bre", GROUP_CH), prm_of("bim", GROUP_CH)], n, (GT, GROUP_CH)))
                for g in range(GT):
                    last = product([hs[:, r, g, :, :] for r in range(2)],
                                   [bc(pw[:, r, STEP - 1::-1, g], 2, GROUP_CH) for r in range(2)],
                                   [bc(bb[:, r, g, :], 1, STEP) for r in range(2)], STEP * GROUP_CH, (STEP, GROUP_CH))
                    if g < GT - 1:
                        ch.link(last)
                last.then_inc(hs_ready, 1)
                dve.wait_ge(hs_ready, i + 1)
                for g in range(GT):
                    c = [prm_of(nm, GROUP_CH)[:, g, :] for nm in ("cre", "cim")]
                    ch.link(product([gg[:, r, g, :, :] for r in range(2)],
                                    [bc(pw[:, r, :, g], 2, GROUP_CH) for r in range(2)],
                                    [bc(x, 1, STEP + 1) for x in c], (STEP + 1) * GROUP_CH, (STEP + 1, GROUP_CH)))
                im = gg[:, 1, :, :, :].rearrange("p g t c -> p (g t c)")
                ts(im, im, -1.0, None, ALU.mult).then_inc(gg_ready, 1)
                ch.mark(dve.tensor_copy(rot[:, 0, :, 1], cs[:, 1, :]))
                ch.mark(dve.tensor_copy(rot[:, 1, :, 1], sn[:, 1, :]))
                ch.link(dve.tensor_copy(decay8[:, :, 1:NBLK], bc(m8, 2, NBLK - 1)))
                for j in range(1, 7):
                    w = 1 << j
                    ch.link(product([rot[:, r, :, w:2 * w] for r in range(2)], [rot[:, r, :, 0:w] for r in range(2)],
                                    [bc(x[:, j + 1, :], 2, w) for x in (cs, sn)], GT * w, (GT, w)))
                dve.wait_ge(k.tile_done, i * tiles + U_ + 1)
                dve.wait_ge(ssm_out, 16 * i)
                s = slot(half, U_)
                tt(uT[:, :], pair[s], rstd[:, :], ALU.mult).then_inc(k.pair_free[s], 1)
                job(K_ROWS)
                dve.tensor_copy(k_rows[:, :, :].rearrange("p (g j) n -> p j g n", j=2),
                                X[0][0:GROUP_CH, :, :].rearrange("p j (g n) -> p j g n", n=P))\
                   .then_inc(k.aux_free[0], 1)
                diag = t1[0:GROUP_CH, 0:GPT * GROUP_CH].rearrange("p (g c) -> p g c", c=GROUP_CH)
                ch.link(tt(diag, bc(k.mats[0:GROUP_CH, IDENT, 0:GROUP_CH], 1, GPT),
                           bc(dm[:, bass.ds(i * GPT, GPT)], 2, GROUP_CH), ALU.mult))
                dve.wait_ge(k.aux_free[0], auxes(i, K_ROWS) + 1)
                tt(k_rows[:, :, 0:GROUP_CH], k_rows[:, :, 0:GROUP_CH], diag, ALU.add).then_inc(rows_ready, 1)

                def rope(t, when, out, ready):
                    dve.wait_ge(raw_ready, 2 * i + when)
                    dve.wait_ge(k.pair_free[slot(half, t)], uses(jj, half, t) + 1)
                    ch.mark(tt(raw[:, :], raw[:, :], cosr[:, :], ALU.mult))
                    ch.link(tt(swap[:, :], swap[:, :], sinr[:, :], ALU.mult))
                    tt(out[:, :], raw[:, :], swap[:, :], ALU.add).then_inc(ready, 1)

                rope(K_, 1, kT, kT_ready)
                dve.wait_ge(k.tile_done, i * tiles + V_ + 1)
                dve.wait_ge(ret_ready, i)
                s = slot(half, V_)
                tt(vT[:, :], pair[s], rstd[:, :], ALU.mult).then_inc(k.pair_free[s], 1)
                job(STATES)
                dve.wait_ge(mT_in, (i + 1) * (16 * STEP))
                xi = [X[1][:, r, :].rearrange("p (g n) -> p g n", n=NBLK) for r in range(2)]
                product([z[:, r, :, :] for r in range(2)], xi, [rot[:, r, :, :] for r in range(2)], GT * NBLK,
                        (GT, NBLK), conj=True).then_inc(k.aux_free[1], 1)
                dve.wait_ge(k.aux_free[1], auxes(i, STATES) + 1)
                w = [t[:, 0:GT * NBLK] for t in (t1, t2)]
                for r in range(2):
                    ch.link(dve.tensor_tensor_scan(w[r], decay8[:, :, :].rearrange("p g n -> p (g n)"),
                                                   z[:, r, :, :].rearrange("p g n -> p (g n)"), 0.0, ALU.mult, ALU.add))
                wv = [x.rearrange("p (g n) -> p g n", n=NBLK)[:, :, 0:NBLK - 1] for x in w]
                zr, zi = (z[:, r, :, 0:NBLK - 1] for r in range(2))
                cr, ci = (rot[:, r, :, 0:NBLK - 1] for r in range(2))
                ch.mark(tt(zr, wv[0], cr, ALU.mult))
                ch.link(tt(zi, wv[1], ci, ALU.mult))
                ch.link(tt(xp[:, 0, :, 1:NBLK], zr, zi, ALU.subtract))
                ch.mark(tt(zr, wv[0], ci, ALU.mult))
                ch.link(tt(zi, wv[1], cr, ALU.mult))
                tt(xp[:, 1, :, 1:NBLK], zr, zi, ALU.add).then_inc(xp_ready, 1)
                rope(Q_, 2, qT, qT_ready)
                dve.wait_ge(qT_ready, i + 1)
                dve.wait_ge(head_in, 16 * (i + 1))
                tt(qxi[:, :].rearrange("p (c t) -> p c t", t=P), qT[:, :].rearrange("p (c t) -> p c t", t=P),
                   bc(hc[:, HC_XI:HC_XI + P], 1, NC), ALU.mult).then_inc(qxi_ready, 1)
                dve.wait_ge(k.tile_done, i * tiles + G_ + 1)
                job(V_TOK)
                s = slot(half, G_)
                tt(vT[:, :], pair[s], rstd[:, :], ALU.mult).then_inc(k.pair_free[s], 1)
                job(KV)
                ch.link(dve.tensor_copy(R[:, 1, :], Xf[0][:, 0:P]))
                for c in range(1, NC - 1):
                    last = stt(out=R[:, c + 1, :], in0=R[:, c, :], scalar=hc[:, HC_GAMMA:HC_GAMMA + 1],
                               in1=Xf[0][:, c * P:(c + 1) * P], op0=ALU.mult, op1=ALU.add)
                    if c < NC - 2:
                        ch.link(last)
                last.then_inc(k.aux_free[0], 1)
                job(SCORES)
                tt(sT[:, :, :], Xf[0].rearrange("p (c t) -> p c t", t=P), bc(hc[:, HC_DECAY:HC_DECAY + P], 1, NC),
                   ALU.mult).then_inc(k.aux_free[0], 1)
                dve.wait_ge(k.aux_free[0], auxes(i, VARIANCE) + 1)
                dve.reciprocal(rcol[:, :], col[:, :]).then_inc(inv_ready, 1)
                job(RSTD)
                dve.wait_ge(gate_ready, i + 1)
                stt(out=yc[:, :], in0=yc[:, :], scalar=k.vecs[:, bass.ds(i + VEC["gn"][0], 1)], in1=Xf[1],
                    op0=ALU.mult, op1=ALU.mult).then_inc(k.aux_free[1], 1)
                dve.wait_ge(k.aux_free[1], auxes(i, RSTD) + 1)
                tt(yc[:, :], yc[:, :], vT[:, :], ALU.mult).then_inc(ret_ready, 1)

            with dve.Fori(0, HEADS // 2) as jj:
                ch.enter(jj, STEP_LINKS)
                step(jj, 0)
                step(jj, 1)
                ch.leave(HEADS // 2)


class Work:
    pass


def open_work(nc, ctx, name):
    w = Work()

    def sb(n, shape, dt=F32):
        return ctx.enter_context(nc.sbuf_tensor(f"{n}_{name}", shape, dt))

    w.a_hi, w.a_lo = sb("a_hi", [P, KT, SEQ], F32R), sb("a_lo", [P, KT, SEQ], F32R)
    w.g_hi, w.g_lo = sb("g_hi", [P, HID, SEQ], F32R), sb("g_lo", [P, HID, SEQ], F32R)
    w.mix = sb("mix", [P, KT, SEQ])
    w.x = sb("x_res", [P, KT, SEQ])
    w.tmp = sb("tmp", [P, 2, SEQ])
    w.acc = sb("acc", [P, SEQ])
    w.col, w.rcol = sb("col", [P, NC]), sb("rcol", [P, NC])
    return w


def signals(nc, ctx, stage, names):
    return {n: ctx.enter_context(nc.semaphore(f"{stage}_{n}")) for n in names.split()}


NORM = "sq added sums root inv row x_new hraw hhi hlo"


def aux(k):
    x = [k.ps[:, 4:6, :], k.ps[:, 6:8, :]]
    return x, [r.rearrange("p a b -> p (a b)") for r in x]


def rstd_pe(pe, k, w, s):
    _, xf = aux(k)
    pe.wait_ge(s["added"], KT)
    for c in range(NC):
        ins = pe.matmul(xf[0][:, c:c + 1], w.acc[:, c * P:(c + 1) * P], k.mean_col[:, :], start=True, stop=True)
    ins.then_inc(s["sums"], 1)
    pe.wait_ge(s["inv"], 1)
    for c in range(NC):
        ins = pe.matmul(xf[1][:, c * P:(c + 1) * P], w.rcol[:, c:c + 1].broadcast_to([P, P]), k.mats[:, IDENT, :],
                        start=True, stop=True)
    ins.then_inc(s["row"], 1)


def squares_act(act, w, s, src, ready):
    for t in range(KT):
        ready(t)
        if t >= 2:
            act.wait_ge(s["added"], t - 1)
        act.activation(w.tmp[:, t % 2, :], src[:, t, :], ACT.Square).then_inc(s["sq"], 1)


def add_square(dve, w, s, t):
    dve.wait_ge(s["sq"], t + 1)
    if t == 0:
        dve.tensor_copy(w.acc[:, :], w.tmp[:, 0, :]).then_inc(s["added"], 1)
    else:
        dve.wait_ge(s["added"], t)
        dve.tensor_tensor(w.acc[:, :], w.acc[:, :], w.tmp[:, t % 2, :], ALU.add).then_inc(s["added"], 1)


def root_act(act, k, w, s):
    _, xf = aux(k)
    act.wait_ge(s["sums"], 1)
    act.activation(w.col[:, :], xf[0][:, 0:NC], ACT.Sqrt, bias=k.eps[:, :]).then_inc(s["root"], 1)


def inverse_dve(dve, w, s):
    dve.wait_ge(s["root"], 1)
    dve.reciprocal(w.rcol[:, :], w.col[:, :]).then_inc(s["inv"], 1)


def residual_dve(dve, k, w, s, chain, gain, after=None):
    _, xf = aux(k)
    dve.wait_ge(s["row"], 1)
    for t in range(KT):
        chain.link(dve.scalar_tensor_tensor(out=w.mix[:, t, :], in0=w.mix[:, t, :], scalar=gain(t), in1=xf[1],
                                            op0=ALU.mult, op1=ALU.mult))
        dve.tensor_tensor(w.x[:, t, :], w.x[:, t, :], w.mix[:, t, :], ALU.add).then_inc(s["x_new"], 1)
        if after:
            after(t)


def split_norm_act(act, w, s, bias):
    for t in range(KT):
        act.wait_ge(s["hraw"], t + 1)
        if bias:
            act.activation(w.a_hi[:, t, :], w.tmp[:, t % 2, :], ACT.Identity, bias=bias(t)).then_inc(s["hhi"], 1)
        else:
            act.activation(w.a_hi[:, t, :], w.tmp[:, t % 2, :], ACT.Copy).then_inc(s["hhi"], 1)


def split_norm_dve(dve, k, w, s, gain, bias):
    _, xf = aux(k)
    dve.wait_ge(s["row"], 1)

    def low(t):
        dve.wait_ge(s["hhi"], t + 1)
        hi = w.a_hi[:, t, :].bitcast(F32)
        if bias:
            dve.scalar_tensor_tensor(out=w.a_lo[:, t, :], in0=w.tmp[:, t % 2, :], scalar=bias(t), in1=hi,
                                     op0=ALU.add, op1=ALU.subtract).then_inc(s["hlo"], 1)
        else:
            dve.tensor_tensor(w.a_lo[:, t, :], w.tmp[:, t % 2, :], hi, ALU.subtract).then_inc(s["hlo"], 1)

    for t in range(KT):
        if t >= 2:
            dve.wait_ge(s["hlo"], t - 1)
        dve.scalar_tensor_tensor(out=w.tmp[:, t % 2, :], in0=w.x[:, t, :], scalar=gain(t), in1=xf[1],
                                 op0=ALU.mult, op1=ALU.mult).then_inc(s["hraw"], 1)
        if t:
            low(t - 1)
    low(KT - 1)


def phase2(nc, k, d, w):
    with ExitStack() as ctx:
        s = signals(nc, ctx, "p2", "ld0 ld1 x_in chain ghi glo mhi mlo b_free yraw yhi ylo")
        r1, r2 = signals(nc, ctx, "p2r", NORM), signals(nc, ctx, "p2n", NORM)
        base = P1_TILES
        out0 = base + GLU_TILES
        X, Xf = aux(k)
        pair = [k.ps[:, 2 * q:2 * q + 2, :].rearrange("p a b -> p (a b)") for q in range(2)]
        ld = [s["ld0"], s["ld1"]]
        block = ctx.enter_context(nc.Block())

        @block.sync
        def _(sp):
            for t in range(2 * HEADS):
                if t >= 2:
                    sp.wait_ge(s["glo"], min(t - 1, HEADS))
                    if t - 1 > HEADS:
                        sp.wait_ge(s["mlo"], t - 1 - HEADS)
                sp.dma_start(w.tmp[:, t % 2, :], d.y_scr[(t + HEADS) % (2 * HEADS), :, :]).then_inc(ld[t % 2], 16)
            sp.dma_start(w.x[:, :, :], d.xT).then_inc(s["x_in"], 16)
            stream_load(sp, k, base + 4, base + P2_TILES + 4)

        @block.gpsimd
        def _(pool):
            stream_split(pool, k, base + 2, base + P2_TILES + 2)

        @block.tensor
        def _(pe):
            pe.wait_ge(s["glo"], HEADS)
            with pe.Fori(0, GLU_TILES // 2) as j:
                for q in range(2):
                    i = 2 * j + q
                    pe.wait_ge(k.w_split, base + i + 1)
                    pe.wait_ge(s["b_free"], i)
                    tile_products(pe, k, q, w.g_hi, w.g_lo,
                                  [(X[0][:, h, :], slice(h * HALF, (h + 1) * HALF)) for h in range(2)], kts=HEADS)
                    pe.wait_ge(k.pair_free[q], base // 2 + j)
                    tile_products(pe, k, q, w.g_hi, w.g_lo, both_halves(k, q), kts=HEADS, at=HEADS * P)\
                        .then_inc(k.tile_done, 1)
            pe.wait_ge(s["mlo"], HEADS)
            pe.wait_ge(s["ylo"], HEADS)
            with pe.Fori(0, KT // 2) as j:
                for q in range(2):
                    gemm(pe, k, out0 + 2 * j + q, q, out0 // 2 + j, w.a_hi, w.a_lo)
            rstd_pe(pe, k, w, r1)
            rstd_pe(pe, k, w, r2)

        @block.scalar
        def _(act):
            for t in range(2 * HEADS):
                act.wait_ge(ld[t % 2], 16 * (t // 2 + 1))
                if t < HEADS:
                    act.activation(w.g_hi[:, t, :], w.tmp[:, t % 2, :], ACT.Copy).then_inc(s["ghi"], 1)
                else:
                    act.activation(w.a_hi[:, t - HEADS, :], w.tmp[:, t % 2, :], ACT.Copy).then_inc(s["mhi"], 1)
            with act.Fori(0, GLU_TILES // 2) as j:
                for q in range(2):
                    i = 2 * j + q
                    act.wait_ge(k.tile_done, base + i + 1)
                    act.wait_ge(s["ylo"], i)
                    act.activation(w.acc[:, :], Xf[0], ACT.Sigmoid).then_inc(s["b_free"], 1)
                    act.wait_ge(k.pair_free[q], base // 2 + j + 1)
                    act.activation(w.a_hi[:, bass.ds(HEADS + i, 1), :].rearrange("p a t -> p (a t)"),
                                   w.mix[:, q, :], ACT.Copy).then_inc(s["yhi"], 1)
            with act.Fori(0, KT // 2) as j:
                for q in range(2):
                    t = 2 * j + q
                    act.wait_ge(k.tile_done, out0 + t + 1)
                    act.activation(w.mix[:, bass.ds(t, 1), :].rearrange("p a t -> p (a t)"), pair[q], ACT.Copy)\
                       .then_inc(s["yraw"], 1)
                    act.wait_ge(r1["added"], 2 * j)
                    act.wait_ge(s["yraw"], t + 1)
                    act.activation(w.tmp[:, q, :], pair[q], ACT.Square).then_inc(k.pair_free[q], 1)
            root_act(act, k, w, r1)
            squares_act(act, w, r2, w.x, lambda t: act.wait_ge(r1["x_new"], t + 1))
            root_act(act, k, w, r2)
            split_norm_act(act, w, r2, None)

        @block.vector
        def _(dve):
            ch = Chain(dve, s["chain"])
            tt = dve.tensor_tensor
            for t in range(2 * HEADS):
                if t < HEADS:
                    dve.wait_ge(s["ghi"], t + 1)
                    tt(w.g_lo[:, t, :], w.tmp[:, t % 2, :], w.g_hi[:, t, :].bitcast(F32), ALU.subtract)\
                        .then_inc(s["glo"], 1)
                else:
                    dve.wait_ge(s["mhi"], t - HEADS + 1)
                    tt(w.a_lo[:, t - HEADS, :], w.tmp[:, t % 2, :], w.a_hi[:, t - HEADS, :].bitcast(F32),
                       ALU.subtract).then_inc(s["mlo"], 1)
            with dve.Fori(0, GLU_TILES // 2) as j:
                for q in range(2):
                    i = 2 * j + q
                    dve.wait_ge(s["b_free"], i + 1)
                    tt(w.mix[:, q, :], pair[q], w.acc[:, :], ALU.mult).then_inc(k.pair_free[q], 1)
                    dve.wait_ge(s["yhi"], i + 1)
                    part = [x[:, bass.ds(HEADS + i, 1), :].rearrange("p a t -> p (a t)") for x in (w.a_hi, w.a_lo)]
                    tt(part[1], w.mix[:, q, :], part[0].bitcast(F32), ALU.subtract).then_inc(s["ylo"], 1)
            dve.wait_ge(s["ylo"], HEADS)
            dve.memset(w.acc[:, :], 0.0).then_inc(s["chain"], 1)
            ch.n += 1
            dve.wait_ge(s["chain"], 1)
            with dve.Fori(0, KT // 2) as j:
                for q in range(2):
                    t = 2 * j + q
                    dve.wait_ge(k.pair_free[q], out0 // 2 + j + 1)
                    dve.wait_ge(r1["added"], t)
                    tt(w.acc[:, :], w.acc[:, :], w.tmp[:, q, :], ALU.add).then_inc(r1["added"], 1)
            inverse_dve(dve, w, r1)
            dve.wait_ge(s["x_in"], 16)
            residual_dve(dve, k, w, r1, ch, lambda t: k.vecs[:, VEC["mix_post"][0] + t:VEC["mix_post"][0] + t + 1],
                         lambda t: add_square(dve, w, r2, t - 1) if t else None)
            add_square(dve, w, r2, KT - 1)
            inverse_dve(dve, w, r2)
            split_norm_dve(dve, k, w, r2, lambda t: k.vecs[:, VEC["mlp_pre"][0] + t:VEC["mlp_pre"][0] + t + 1], None)


def mlp_phase(nc, k, d, w, base, gain, name, ada_from=None, out=None):
    with ExitStack() as ctx:
        s = signals(nc, ctx, name, "relu square hhi hlo cleared chain ada_in out")
        xs = [ctx.enter_context(nc.semaphore(f"{name}_aux_free{q}")) for q in range(2)]
        ada_done = ctx.enter_context(nc.semaphore(f"{name}_ada_done"))
        r = signals(nc, ctx, name + "r", NORM)
        X, Xf = aux(k)
        pair = [k.ps[:, 2 * q:2 * q + 2, :].rearrange("p a b -> p (a b)") for q in range(2)]
        steps, per = MLP_STEPS, 2 * HID
        last = base + MLP_TILES
        A = HID // 2 if ada_from is not None else 0
        per_aux = HID // 2 + A
        block = ctx.enter_context(nc.Block())

        @block.sync
        def _(sp):
            stream_load(sp, k, base + 4, min(last + 4, ALL_TILES))
            if out is not None:
                for t in range(KT):
                    sp.wait_ge(r["x_new"], t + 1)
                    sp.dma_start(out[:, t, :], w.x[:, t, :]).then_inc(s["out"], 16)
                sp.wait_ge(s["out"], 16 * KT)

        @block.gpsimd
        def _(pool):
            stream_split(pool, k, base + 2, min(last + 2, ALL_TILES))

        @block.tensor
        def _(pe):
            with pe.Fori(0, steps) as i:
                n = base + i * per
                for t in range(HID):
                    gemm(pe, k, n + t, t % 2, base // 2 + i * (per // 2) + t // 2, w.a_hi, w.a_lo)
                    if A:
                        pe.wait_ge(s["ada_in"], (i * HID + t + 1) * 16)
                        pe.wait_ge(xs[t % 2], i * per_aux + t // 2)
                        ada_products(pe, k, X[t % 2][:, 0, :]).then_inc(ada_done, 1)
                for t in range(HID):
                    q = t % 2
                    pe.wait_ge(k.w_split, n + HID + t + 1)
                    pe.wait_ge(k.pair_free[q], base // 2 + i * (per // 2) + (HID + t) // 2)
                    pe.wait_ge(xs[q], i * per_aux + A + t // 2)
                    for half, banks in ((0, both_halves(k, q)),
                                        (1, [(X[q][:, h, :], slice(h * HALF, (h + 1) * HALF)) for h in range(2)])):
                        for kt in range(HID):
                            if t == 0 and half == 0:
                                pe.wait_ge(s["hlo"], i * HID + kt + 1)
                            c = slice((half * HID + kt) * P, (half * HID + kt + 1) * P)
                            ins = products(pe, k.w_hi[:, q, c], k.w_lo[:, q, c], w.g_hi[:, kt, :], w.g_lo[:, kt, :],
                                           banks, kt == 0, kt == HID - 1)
                    ins.then_inc(k.tile_done, 1)
            rstd_pe(pe, k, w, r)

        @block.scalar
        def _(act):
            if A:
                act.dma_start(k.ada_w[:, :], d.ada_w[ada_from, :, :]).then_inc(s["ada_in"], 16)
            with act.Fori(0, steps) as i:
                n = base + i * per
                for t in range(HID):
                    act.wait_ge(k.tile_done, n + t + 1)
                    if t >= 2:
                        act.wait_ge(s["hlo"], i * HID + t - 1)
                    else:
                        act.wait_ge(s["hlo"], i * HID)
                    act.activation(w.tmp[:, t % 2, :], pair[t % 2], ACT.Relu).then_inc(k.pair_free[t % 2], 1)
                    if A:
                        index = i * HID + t
                        act.wait_ge(ada_done, index + 1)
                        act.activation(k.ada[:, bass.ds(index + ada_from, 1), :].rearrange("p a c -> p (a c)"),
                                       X[t % 2][:, 0, 0:2], ACT.Copy).then_inc(xs[t % 2], 1)
                        act.dma_start(k.ada_w[:, :], d.ada_w[bass.ds(index + ada_from + 1, 1), :, :]
                                      .rearrange("a p c -> p (a c)")).then_inc(s["ada_in"], 16)
                    act.wait_ge(s["square"], i * HID + t + 1)
                    act.activation(w.g_hi[:, t, :], w.tmp[:, t % 2, :], ACT.Copy).then_inc(s["hhi"], 1)
            if A:
                act.wait_ge(s["ada_in"], (steps * HID + 1) * 16)
            act.wait_ge(xs[1], steps * per_aux)
            act.wait_ge(k.pair_free[1], last // 2)
            act.wait_ge(xs[0], steps * per_aux)
            act.wait_ge(k.pair_free[0], last // 2)
            squares_act(act, w, r, w.mix, lambda t: None)
            root_act(act, k, w, r)

        @block.vector
        def _(dve):
            ch = Chain(dve, s["chain"])
            tt = dve.tensor_tensor
            dve.memset(w.mix[:, :, :], 0.0).then_inc(s["cleared"], 1)
            dve.wait_ge(s["cleared"], 1)
            with dve.Fori(0, steps) as i:
                n = base + i * per
                for t in range(HID):
                    dve.wait_ge(k.pair_free[t % 2], base // 2 + i * (per // 2) + t // 2 + 1)
                    tt(w.tmp[:, t % 2, :], w.tmp[:, t % 2, :], w.tmp[:, t % 2, :], ALU.mult).then_inc(s["square"], 1)
                    dve.wait_ge(s["hhi"], i * HID + t + 1)
                    tt(w.g_lo[:, t, :], w.tmp[:, t % 2, :], w.g_hi[:, t, :].bitcast(F32), ALU.subtract)\
                        .then_inc(s["hlo"], 1)
                for t in range(HID):
                    q = t % 2
                    dve.wait_ge(k.tile_done, n + HID + t + 1)
                    if t == 0:
                        dve.wait_ge(k.pair_free[1], base // 2 + i * (per // 2))
                        dve.wait_ge(xs[1], i * per_aux)
                    tt(w.mix[:, 2 * t, :], w.mix[:, 2 * t, :], pair[q], ALU.add).then_inc(k.pair_free[q], 1)
                    tt(w.mix[:, 2 * t + 1, :], w.mix[:, 2 * t + 1, :], Xf[q], ALU.add).then_inc(xs[q], 1)
            for t in range(KT):
                add_square(dve, w, r, t)
            inverse_dve(dve, w, r)
            residual_dve(dve, k, w, r, ch, gain)


ALL_C = NC + CC
XS0 = 4
PAD = TAPS // 2
RAW_X, RAW_C = 0, SEQ + 2 * PAD
RAW_COLS = TOK2 + 4 * PAD
CONV_COLS = RAW_COLS - 2 * PAD
CV_C = RAW_C
MOD_AX, MOD_BX, MOD_AC, MOD_BC, MOD_G1, MOD_A2, MOD_B2, MOD_G2 = range(8)


class Scan:
    pass


def open_scan(nc, ctx):
    v = Scan()

    def sb(n, shape, dt=F32):
        return ctx.enter_context(nc.sbuf_tensor(n, shape, dt))

    v.a_hi, v.a_lo = sb("h2_hi", [P, KT, SEQ], F32R), sb("h2_lo", [P, KT, SEQ], F32R)
    v.tok = sb("tok", [P, ALL_C, (XBC_TILES - 2) * P])
    v.bc = sb("bcT", [P, 4, TOK2])
    v.dt, v.dta = sb("dt", [P, ALL_C, 32]), sb("dta", [P, ALL_C, 32])
    v.acs, v.e_acs = sb("acs", [P, ALL_C, 32]), sb("e_acs", [P, ALL_C, 32])
    v.e_tot, v.w_st = sb("e_tot", [P, ALL_C, 32]), sb("w_st", [P, ALL_C, 32])
    v.rows = sb("head_rows", [P, 80])
    return v


def phase4(nc, k, d, v):
    with ExitStack() as ctx:
        def sb(n, shape, dt=F32):
            return ctx.enter_context(nc.sbuf_tensor(n, shape, dt))

        c_hi, c_lo = sb("hc_hi", [P, KT, CTX], F32R), sb("hc_lo", [P, KT, CTX], F32R)
        raw = sb("raw4", [P, RAW_COLS])
        cv = sb("cv4", [P, 2, CONV_COLS])
        wdt_raw = k.ada_w[:, 0:KT * 32].rearrange("p (t h) -> p t h", h=32)
        wdt_hi, wdt_lo = sb("wdt_hi", [P, KT, 32], F32R), sb("wdt_lo", [P, KT, 32], F32R)
        col, rcol = sb("col4", [P, ALL_C]), sb("rcol4", [P, ALL_C])
        md = k.ada_w[:, KT * 32:KT * 32 + 96].rearrange("p (m w) -> p m w", w=2)
        spl = v.bc[:, 0, 0:3 * ALL_C * 32].rearrange("p (j n) -> p j n", j=3)
        xall = v.tok[:, 0:KT, :]
        acc = raw[:, 0:TOK2]
        s = signals(nc, ctx, "p4", "const x_in mod chain sq added sums root inv row hraw hhi hlo wdt_hi wdt_ready "
                                   "dt_raw dt_abs dt_exp dta_ready acs_mm tot_mm dt_done a_exp e_ready evac_ready "
                                   "raw_ready conv silu padded t_done0 t_done1 t_free0 t_free1")
        B0 = P1_TILES + P2_TILES + MLP_TILES
        regions = [k.ps[:, 3 * q:3 * q + 3, :].rearrange("p a b -> p (a b)") for q in range(2)]
        row3 = k.ps[:, 3:6, :].rearrange("p a b -> p (a b)")[:, 0:TOK2]
        PAIRS = (XBC_TILES - XS0) // 2
        t_done, t_free = [s["t_done0"], s["t_done1"]], [s["t_free0"], s["t_free1"]]
        ident = k.mats[:, IDENT, :]
        block = ctx.enter_context(nc.Block())

        def a_part(t, ctx_part):
            return (c_hi if ctx_part else v.a_hi)[:, t, :], (c_lo if ctx_part else v.a_lo)[:, t, :]

        @block.sync
        def _(sp):
            sp.dma_start(xall[:, :, 0:SEQ], d.x2_scr).then_inc(s["x_in"], 16)
            sp.dma_start(xall[:, :, SEQ:TOK2], d.ctxT).then_inc(s["x_in"], 16)
            sp.dma_start(v.rows[:, :], d.head_rows).then_inc(s["const"], 16)
            sp.dma_start(wdt_raw[:, :, :], d.w_dt).then_inc(s["const"], 16)
            stream_load(sp, k, B0 + 4, XBC_END + 4)

        @block.gpsimd
        def _(pool):
            stream_split(pool, k, B0 + 2, XBC_END + 2)

        @block.tensor
        def _(pe):
            pe.wait_ge(s["added"], KT)
            for c in range(ALL_C):
                ins = pe.matmul(k.ps[:, 7, c:c + 1], acc[:, c * P:(c + 1) * P], k.mean_col[:, :], start=True, stop=True)
            ins.then_inc(s["sums"], 1)
            pe.wait_ge(s["inv"], 1)
            for c in range(ALL_C):
                ins = pe.matmul(row3[:, c * P:(c + 1) * P], rcol[:, c:c + 1].broadcast_to([P, P]), ident,
                                start=True, stop=True)
            ins.then_inc(s["row"], 1)
            pe.wait_ge(s["hlo"], 2 * KT)
            pe.wait_ge(s["wdt_ready"], 1)
            for c in range(ALL_C):
                hi, lo = (v.a_hi, v.a_lo) if c < NC else (c_hi, c_lo)
                at = slice(c % NC * P, c % NC * P + P)
                out = k.ps[:, 6, c * 32:(c + 1) * 32]
                for kt in range(KT):
                    pe.matmul(out, hi[:, kt, at], wdt_hi[:, kt, :], start=kt == 0, stop=False)
                    pe.matmul(out, hi[:, kt, at], wdt_lo[:, kt, :], start=False, stop=False)
                    ins = pe.matmul(out, lo[:, kt, at], wdt_hi[:, kt, :], start=False, stop=kt == KT - 1)
            ins.then_inc(s["dt_raw"], 1)

            def tile(n, q, uses):
                pe.wait_ge(k.w_split, n + 1)
                pe.wait_ge(k.pair_free[q], uses)
                for kt in range(KT):
                    c = slice(kt * P, (kt + 1) * P)
                    wh, wl = k.w_hi[:, q, c], k.w_lo[:, q, c]
                    outs = [(regions[q][:, h * HALF:(h + 1) * HALF], slice(h * HALF, (h + 1) * HALF)) for h in range(2)]
                    products(pe, wh, wl, v.a_hi[:, kt, :], v.a_lo[:, kt, :], outs, kt == 0, kt == KT - 1)
                    ins = products(pe, wh, wl, c_hi[:, kt, :], c_lo[:, kt, :],
                                   [(regions[q][:, SEQ:TOK2], slice(0, CTX))], kt == 0, kt == KT - 1)
                ins.then_inc(k.tile_done, 1)

            def transposes(j, q, src, first):
                for m, cs in enumerate((range(0, 4), range(4, 8), range(8, 10))):
                    b = (3 * q + m) % 2
                    pe.wait_ge(t_free[b], 3 * j + (3 * q + m) // 2)
                    for c in cs:
                        at = c * P + (CV_C - SEQ if c >= NC and first else 0)
                        ins = pe.transpose(k.ps[:, 6 + b, (c % 4) * P:(c % 4 + 1) * P], src[:, at:at + P], ident)
                    ins.then_inc(t_done[b], 1)

            n = B0
            for q in range(2):
                tile(n + q, q, n // 2)
            pe.wait_ge(s["dta_ready"], 1)
            pe.matmul(k.ps[:, 6, 0:160], k.mats[:, TRI_LE, :], v.dta[:, :, 0:16], start=True, stop=True)
            pe.matmul(k.ps[:, 6, 160:320], k.mats[:, TRI_GE, :], v.dta[:, :, 16:32], start=True, stop=True)\
              .then_inc(s["acs_mm"], 1)
            pe.matmul(k.ps[:, 7, 0:320], k.mean_col[:, 0:1].broadcast_to([P, P]), v.dta[:, :, :].rearrange("p c h -> p (c h)"),
                      start=True, stop=True).then_inc(s["tot_mm"], 1)
            for q in range(2):
                tile(n + 2 + q, q, n // 2 + 1)
            pe.wait_ge(s["e_ready"], 2)
            for q in range(2):
                pe.wait_ge(s["silu"], 2 * (q + 1))
                transposes(0, q, v.bc[:, q, :], False)

            def value_transposes(j):
                for q in range(2):
                    pe.wait_ge(s["silu"], 2 * (XS0 + 2 * j + q + 1))
                    transposes(j + 1, q, cv[:, q, :], True)

            for q in range(2):
                tile(n + XS0 + q, q, n // 2 + XS0 // 2)
            with pe.Fori(0, PAIRS - 1) as j:
                tile(n + XS0 + 2 + 2 * j, 0, n // 2 + XS0 // 2 + 1 + j)
                value_transposes(j)
                tile(n + XS0 + 3 + 2 * j, 1, n // 2 + XS0 // 2 + 1 + j)
            value_transposes(PAIRS - 1)

        @block.scalar
        def _(act):
            for t in range(KT):
                if t == 0:
                    act.wait_ge(s["x_in"], 32)
                if t >= 2:
                    act.wait_ge(s["added"], t - 1)
                act.activation(cv[:, t % 2, 0:TOK2], xall[:, t, :], ACT.Square).then_inc(s["sq"], 1)
            act.wait_ge(s["sums"], 1)
            act.activation(col[:, :], k.ps[:, 7, 0:ALL_C], ACT.Sqrt, bias=k.eps[:, :]).then_inc(s["root"], 1)
            act.wait_ge(s["const"], 32)
            act.activation(wdt_hi[:, :, :], wdt_raw[:, :, :], ACT.Copy).then_inc(s["wdt_hi"], 1)
            for t in range(KT):
                for part, cols, m in ((0, slice(0, SEQ), MOD_BX), (1, slice(SEQ, TOK2), MOD_BC)):
                    act.wait_ge(s["hraw"], 2 * t + part + 1)
                    act.activation(a_part(t, part)[0], cv[:, t % 2, cols], ACT.Identity, bias=k.mod[:, m, t:t + 1])\
                       .then_inc(s["hhi"], 1)
            act.wait_ge(s["dt_abs"], 1)
            act.activation(spl[:, 1, :], spl[:, 1, :], ACT.Exp).then_inc(s["dt_exp"], 1)
            act.activation(v.rows[:, 32:64], v.rows[:, 32:64], ACT.Exp).then_inc(s["a_exp"], 1)

            def raw_out(n, q, j2):
                act.wait_ge(k.tile_done, n + 1)
                act.wait_ge(s["conv"], j2)
                act.activation(raw[:, RAW_X + PAD:RAW_X + PAD + SEQ], regions[q][:, 0:SEQ], ACT.Copy)\
                   .then_inc(s["raw_ready"], 1)
                act.wait_ge(s["raw_ready"], j2 + 1)
                act.activation(raw[:, RAW_C + PAD:RAW_C + PAD + CTX], regions[q][:, SEQ:TOK2], ACT.Copy)\
                   .then_inc(k.pair_free[q], 1)

            def silu_out(j2, q, x_out, c_out):
                act.wait_ge(s["conv"], j2 + 1)
                act.activation(x_out, cv[:, q, 0:SEQ], ACT.Silu).then_inc(s["silu"], 1)
                act.activation(c_out, cv[:, q, CV_C:CV_C + CTX], ACT.Silu).then_inc(s["silu"], 1)

            def token_rows(j, q, cols):
                for m, (c0, c1) in enumerate(((0, 4), (4, 8), (8, 10))):
                    b = (3 * q + m) % 2
                    act.wait_ge(t_done[b], 3 * j + (3 * q + m) // 2 + 1)
                    act.activation(v.tok[:, c0:c1, cols], k.ps[:, 6 + b, 0:(c1 - c0) * P]
                                   .rearrange("p (c n) -> p c n", n=P), ACT.Copy).then_inc(t_free[b], 1)

            act.wait_ge(s["padded"], 1)
            for i in range(2):
                raw_out(B0 + i, i % 2, i)
                silu_out(i, i % 2, v.bc[:, i, 0:SEQ], v.bc[:, i, SEQ:TOK2])
            act.wait_ge(s["dt_done"], 1)
            act.activation(v.e_acs[:, :, :], v.acs[:, :, :], ACT.Exp).then_inc(s["evac_ready"], 1)
            act.activation(v.w_st[:, :, :], v.w_st[:, :, :], ACT.Exp).then_inc(s["evac_ready"], 1)
            act.activation(v.e_tot[:, :, :].rearrange("p c h -> p (c h)"), k.ps[:, 7, 0:320], ACT.Exp, scale=1.0 * D_MODEL)\
               .then_inc(s["e_ready"], 1)
            for i in range(2, 4):
                raw_out(B0 + i, i % 2, i)
                silu_out(i, i % 2, v.bc[:, i, 0:SEQ], v.bc[:, i, SEQ:TOK2])
            for q in range(2):
                token_rows(0, q, slice(q * P, (q + 1) * P))

            def value_tile(i, q, between=None):
                raw_out(B0 + i, q, i)
                if between:
                    between()
                silu_out(i, q, cv[:, q, 0:SEQ], cv[:, q, CV_C:CV_C + CTX])

            def value_rows(j):
                for q in range(2):
                    token_rows(j + 1, q, bass.ds((2 * j + q + 2) * P, P))

            for q in range(2):
                value_tile(XS0 + q, q)
            with act.Fori(0, PAIRS - 1) as j:
                value_tile(XS0 + 2 + 2 * j, 0, lambda: value_rows(j))
                value_tile(XS0 + 3 + 2 * j, 1)
            value_rows(PAIRS - 1)

        @block.vector
        def _(dve):
            ch = Chain(dve, s["chain"])
            tt, ts, stt = dve.tensor_tensor, dve.tensor_scalar, dve.scalar_tensor_tensor
            a, b = VEC["b_ada"]
            ch.link(tt(md[:, :, :], k.ada[:, :, :], bc(k.vecs[:, a:b], 2, 2), ALU.add))
            for m, first, who, norm in ((MOD_AX, 8, 0, "mix_pre2"), (MOD_AC, 8, 1, "mix_pre2"), (MOD_A2, 32, 0, "mlp_pre2")):
                g = slice(*VEC[norm])
                ch.link(stt(out=k.mod[:, m, :], in0=md[:, first:first + KT, who], scalar=1.0, in1=k.vecs[:, g],
                            op0=ALU.add, op1=ALU.mult))
            for m, first, who in ((MOD_BX, 0, 0), (MOD_BC, 0, 1), (MOD_B2, 24, 0)):
                ch.link(dve.tensor_copy(k.mod[:, m, :], md[:, first:first + KT, who]))
            for m, first, norm in ((MOD_G1, 16, "mix_post2"), (MOD_G2, 40, "mlp_post2")):
                ch.link(tt(k.mod[:, m, :], md[:, first:first + KT, 0], k.vecs[:, slice(*VEC[norm])], ALU.mult))
            for t in range(KT):
                dve.wait_ge(s["sq"], t + 1)
                if t == 0:
                    dve.tensor_copy(acc, cv[:, 0, 0:TOK2]).then_inc(s["added"], 1)
                else:
                    dve.wait_ge(s["added"], t)
                    tt(acc, acc, cv[:, t % 2, 0:TOK2], ALU.add).then_inc(s["added"], 1)
            dve.wait_ge(s["root"], 1)
            dve.reciprocal(rcol[:, :], col[:, :]).then_inc(s["inv"], 1)
            dve.wait_ge(s["wdt_hi"], 1)
            tt(wdt_lo[:, :, :], wdt_raw[:, :, :], wdt_hi[:, :, :].bitcast(F32), ALU.subtract).then_inc(s["wdt_ready"], 1)
            dve.wait_ge(s["row"], 1)

            def low(t):
                for part, cols, m in ((0, slice(0, SEQ), MOD_BX), (1, slice(SEQ, TOK2), MOD_BC)):
                    dve.wait_ge(s["hhi"], 2 * t + part + 1)
                    hi, lo = a_part(t, part)
                    stt(out=lo, in0=cv[:, t % 2, cols], scalar=k.mod[:, m, t:t + 1], in1=hi.bitcast(F32),
                        op0=ALU.add, op1=ALU.subtract).then_inc(s["hlo"], 1)

            for t in range(KT):
                if t >= 2:
                    dve.wait_ge(s["hlo"], 2 * (t - 1))
                for cols, m in ((slice(0, SEQ), MOD_AX), (slice(SEQ, TOK2), MOD_AC)):
                    stt(out=cv[:, t % 2, cols], in0=xall[:, t, cols], scalar=k.mod[:, m, t:t + 1], in1=row3[:, cols],
                        op0=ALU.mult, op1=ALU.mult).then_inc(s["hraw"], 1)
                if t:
                    low(t - 1)
            low(KT - 1)
            dve.wait_ge(s["hlo"], 2 * KT)
            dve.memset(raw[:, :], 0.0).then_inc(s["padded"], 1)
            dve.wait_ge(s["const"], 32)
            dve.wait_ge(s["dt_raw"], 1)
            x, e, u = (spl[:, j, :] for j in range(3))
            xv = x.rearrange("p (c h) -> p c h", h=32)
            ch.link(tt(xv, k.ps[:, 6, 0:320].rearrange("p (c h) -> p c h", h=32), bc(v.rows[:, 0:32], 1, ALL_C), ALU.add))
            stt(out=e, in0=x, scalar=-1.0, in1=x, op0=ALU.mult, op1=ALU.min).then_inc(s["dt_abs"], 1)
            dve.wait_ge(s["dt_abs"], 1)
            dve.wait_ge(s["dt_exp"], 1)
            ch.link(ts(u, e, 2.0, None, ALU.add))
            ch.link(dve.reciprocal(u, u))
            ch.link(tt(u, u, e, ALU.mult))
            ch.link(tt(e, u, u, ALU.mult))
            poly = v.w_st[:, :, :].rearrange("p c h -> p (c h)")
            ch.link(ts(poly, e, 2.0 / 17, 2.0 / 15, ALU.mult, ALU.add))
            for m in (13, 11, 9, 7, 5, 3, 1):
                ch.link(tt(poly, poly, e, ALU.mult))
                ch.link(ts(poly, poly, 2.0 / m, None, ALU.add))
            ch.link(tt(poly, poly, u, ALU.mult))
            ch.link(ts(x, x, 0.0, None, ALU.max))
            ch.link(tt(v.dt[:, :, :].rearrange("p c h -> p (c h)"), x, poly, ALU.add))
            dve.wait_ge(s["a_exp"], 1)
            tt(v.dta[:, :, :], v.dt[:, :, :], bc(v.rows[:, 32:64], 1, ALL_C), ALU.mult).then_inc(s["chain"], 1)
            ch.n += 1
            dve.wait_ge(s["chain"], ch.n)
            ts(v.dta[:, :, :], v.dta[:, :, :], -1.0, None, ALU.mult).then_inc(s["dta_ready"], 1)

            def convolve(i, q, tap, bias, evacuated):
                dve.wait_ge(s["raw_ready"], i + 1)
                dve.wait_ge(k.pair_free[q], evacuated)
                ch.link(ts(cv[:, q, :], raw[:, 0:CONV_COLS], tap(0), bias, ALU.mult, ALU.add))
                for m in range(1, TAPS):
                    ins = stt(out=cv[:, q, :], in0=raw[:, m:m + CONV_COLS], scalar=tap(m), in1=cv[:, q, :],
                              op0=ALU.mult, op1=ALU.add)
                    if m < TAPS - 1:
                        ch.link(ins)
                ins.then_inc(s["conv"], 1)

            w0, b0 = VEC["conv_w"][0], VEC["conv_b"][0]

            def first_tiles(i):
                if i >= 2:
                    dve.wait_ge(s["silu"], 2 * (i - 1))
                convolve(i, i % 2, lambda m: k.vecs[:, w0 + TAPS * i + m:w0 + TAPS * i + m + 1],
                         k.vecs[:, b0 + i:b0 + i + 1], B0 // 2 + i // 2 + 1)

            dve.wait_ge(s["padded"], 1)
            first_tiles(0)
            first_tiles(1)
            dve.wait_ge(s["acs_mm"], 1)
            for r in range(2):
                ch.link(dve.tensor_copy(v.acs[:, :, 16 * r:16 * r + 16], k.ps[:, 6, 160 * r:160 * r + 160]
                                        .rearrange("p (c h) -> p c h", h=16)))
            dve.wait_ge(s["tot_mm"], 1)
            stt(out=v.w_st[:, :, :], in0=k.ps[:, 7, 0:320].rearrange("p (c h) -> p c h", h=32), scalar=1.0 * D_MODEL,
                in1=v.acs[:, :, :], op0=ALU.mult, op1=ALU.subtract).then_inc(s["dt_done"], 1)
            dve.wait_ge(s["evac_ready"], 2)
            tt(v.w_st[:, :, :], v.w_st[:, :, :], v.dt[:, :, :], ALU.mult).then_inc(s["e_ready"], 1)
            first_tiles(2)
            first_tiles(3)
            with dve.Fori(0, PAIRS) as j:
                ch.enter(j, 2 * (TAPS - 1))
                for q in range(2):
                    i = XS0 + 2 * j + q
                    dve.wait_ge(s["silu"], 2 * (i - 1))
                    dve.wait_ge(t_done[q], 3 * j + 2 + q)
                    convolve(i, q, lambda m, i=i: k.vecs[:, bass.ds(i * TAPS + (w0 + m), 1)],
                             k.vecs[:, bass.ds(i + b0, 1)], B0 // 2 + XS0 // 2 + 1 + j)
                ch.leave(PAIRS)


def phase5(nc, k, d, v):
    with ExitStack() as ctx:
        def sb(n, shape, dt=F32):
            return ctx.enter_context(nc.sbuf_tensor(n, shape, dt))

        state, y, lhs0, xw = (sb(n, [P, SEQ]) for n in ("state5", "y5", "lhs5", "xw5"))
        E = sb("E5", [P, 3, SEQ])
        BT, CT, Bt = (sb(n, [P, NGRP, P]) for n in ("BT_cur", "CT_cur", "Bt_cur"))
        cbm = sb("cbm", [P, 2, NGRP, P])
        lhs = [lhs0, xw]
        stage = k.ada_w
        s = signals(nc, ctx, "p5", "chain cur xw_ready lhs_ready off_added w_ready y_ready y_out y_in u_out x_done "
                                   "x_free0 x_free1 first")
        x_free = [s["x_free0"], s["x_free1"]]
        X, Xf = aux(k)
        pair = [k.ps[:, 2 * q:2 * q + 2, :].rearrange("p a b -> p (a b)") for q in range(2)]
        VAL = NGRP * P
        BWD_JOBS, J = 2, 8
        CB, OFF, F0, B0, F1, B1, ST, DIAG = range(J)
        back = CC
        fwd_ctx = back + BWD_JOBS * NC
        fwd = fwd_ctx + CC
        block = ctx.enter_context(nc.Block())

        def chunk(buf, c, cols):
            return buf[:, bass.ds(c, 1), cols].rearrange("p a n -> p (a n)")

        def heads(ap):
            return ap.rearrange("p (h n) -> p h n", h=SSM_HEADS)

        def per_head(buf, c, r, n=HDIM):
            return bc(chunk(buf, c, slice(SSM_HEADS * r, SSM_HEADS * (r + 1))), 2, n)

        @block.sync
        def _(sp):
            stream_load(sp, k, XBC_END + 4, UZ_END + 4)

        @block.gpsimd
        def _(pool):
            stream_split(pool, k, XBC_END + 2, UZ_END + 2)

        @block.tensor
        def _(pe):
            def add_state(out, b_rows, g):
                return pe.matmul(out[:, g, :], b_rows, xw[:, g * HALF:(g + 1) * HALF], start=True, stop=True)

            def ctx_states(weights, cs):
                for m, c in enumerate(cs):
                    pe.wait_ge(s["xw_ready"], weights + m + 1)
                    for g in range(NGRP):
                        ins = add_state(X[m], v.tok[:, c, g * P:(g + 1) * P], g)
                    ins.then_inc(s["x_done"], 1)

            def off(q):
                for g in range(NGRP):
                    ins = pe.matmul(X[q][:, g, :], CT[:, g, :], state[:, g * HALF:(g + 1) * HALF], start=True, stop=True)
                ins.then_inc(s["x_done"], 1)

            ctx_states(0, (ALL_C - 1, ALL_C - 2))
            with pe.Fori(0, NC) as i:
                pe.wait_ge(s["cur"], 2 * i + 2)
                pe.wait_ge(x_free[0], back // 2 + i)
                pe.wait_ge(x_free[1], back // 2 + i)
                off(0)
                pe.wait_ge(s["xw_ready"], CC + i + 1)
                for g in range(NGRP):
                    ins = add_state(X[1], Bt[:, g, :], g)
                ins.then_inc(s["x_done"], 1)
            pe.wait_ge(x_free[0], fwd_ctx // 2)
            pe.wait_ge(x_free[1], fwd_ctx // 2)
            ctx_states(CC + NC, (NC, NC + 1))

            with pe.Fori(0, NC) as i:
                def job(j):
                    pe.wait_ge(x_free[j % 2], (fwd + j) // 2 + i * (J // 2))

                def decays(j, number, tri):
                    job(j)
                    pe.wait_ge(s["lhs_ready"], 4 * i + number + 1)
                    for h in range(HPG):
                        c = slice(h * P, (h + 1) * P)
                        ins = pe.matmul(Xf[j % 2][:, c], lhs[j % 2][:, c], k.mats[:, tri, :], start=True, stop=True)
                    ins.then_inc(s["x_done"], 1)

                job(CB)
                pe.wait_ge(s["cur"], 2 * NC + 3 * i + 3)
                for g in range(NGRP):
                    ins = pe.matmul(X[0][:, 0, g * P:(g + 1) * P], BT[:, g, :], CT[:, g, :], start=True, stop=True)
                ins.then_inc(s["x_done"], 1)
                job(OFF)
                off(1)
                decays(F0, 0, TRI_LE)
                decays(B0, 1, TRI_GE)
                gemm(pe, k, XBC_END + 2 * i, 0, XBC_END // 2 + i, v.a_hi, v.a_lo)
                decays(F1, 2, TRI_LE)
                decays(B1, 3, TRI_GE)
                gemm(pe, k, XBC_END + 2 * i + 1, 1, XBC_END // 2 + i, v.a_hi, v.a_lo)
                job(ST)
                pe.wait_ge(s["xw_ready"], 2 * CC + NC + i + 1)
                for g in range(NGRP):
                    ins = add_state(X[0], Bt[:, g, :], g)
                ins.then_inc(s["x_done"], 1)
                job(DIAG)
                for h in range(SSM_HEADS):
                    if h % HPG == 0:
                        pe.wait_ge(s["w_ready"], 2 * i + h // HPG + 1)
                    W = E[:, 2 * (h // HPG), :]
                    ins = pe.matmul(Xf[1][:, h * HDIM:(h + 1) * HDIM], W[:, (h % HPG) * P:(h % HPG + 1) * P],
                                    chunk(v.tok, i, slice(VAL + h * HDIM, VAL + (h + 1) * HDIM)), start=True, stop=True)
                ins.then_inc(s["x_done"], 1)

        @block.scalar
        def _(act):
            def current(buf, src):
                act.activation(buf[:, :, :], src, ACT.Copy).then_inc(s["cur"], 1)

            def b_rows(c):
                return chunk(v.tok, c, slice(0, VAL)).rearrange("p (g n) -> p g n", g=NGRP)

            with act.Fori(0, NC) as i:
                c = NC - 1 - i
                act.wait_ge(s["x_done"], back + BWD_JOBS * i)
                current(CT, v.bc[:, NGRP:2 * NGRP, bass.ds(c * P, P)])
                current(Bt, b_rows(c))
                act.wait_ge(s["y_ready"], i + 1)
                act.dma_start(d.y_tok[bass.ds(c, 1), :, :].rearrange("a p n -> p (a n)"), y[:, :]).then_inc(s["y_out"], 16)
            with act.Fori(0, NC) as i:
                act.wait_ge(s["x_done"], fwd + J * i)
                current(BT, v.bc[:, 0:NGRP, bass.ds(i * P, P)])
                current(CT, v.bc[:, NGRP:2 * NGRP, bass.ds(i * P, P)])
                current(Bt, b_rows(i))
                act.wait_ge(s["y_out"], 16 * NC + 16 * i)
                act.dma_start(y[:, :], d.y_tok[bass.ds(i, 1), :, :].rearrange("a p n -> p (a n)")).then_inc(s["y_in"], 16)

                def exps(j, to):
                    act.wait_ge(s["x_done"], fwd + J * i + j + 1)
                    act.activation(E[:, to, :], Xf[j % 2], ACT.Exp).then_inc(x_free[j % 2], 1)

                def staged(q, func, out):
                    act.wait_ge(k.tile_done, XBC_END + 2 * i + q + 1)
                    act.wait_ge(s["u_out"], 16 * (2 * i + q))
                    act.activation(stage[:, :], pair[q], func).then_inc(k.pair_free[q], 1)
                    act.wait_ge(k.pair_free[q], XBC_END // 2 + i + 1)
                    act.dma_start(out[bass.ds(i, 1), :, :].rearrange("a p n -> p (a n)"), stage[:, :])\
                       .then_inc(s["u_out"], 16)

                exps(F0, 0)
                act.wait_ge(s["off_added"], i + 1)
                exps(B0, 1)
                staged(0, ACT.Copy, d.u_scr)
                exps(F1, 2)
                act.wait_ge(s["w_ready"], 2 * i + 1)
                exps(B1, 1)
                staged(1, ACT.Silu, d.z_scr)
                act.wait_ge(s["y_ready"], NC + i + 1)
                act.dma_start(d.y_tok[bass.ds(i, 1), :, :].rearrange("a p n -> p (a n)"), y[:, :]).then_inc(s["y_out"], 16)
            act.wait_ge(s["y_out"], 16 * 2 * NC)
            act.wait_ge(s["u_out"], 16 * 2 * NC)

        @block.vector
        def _(dve):
            ch = Chain(dve, s["chain"])
            tt = dve.tensor_tensor

            def weigh(c, r):
                tt(heads(xw[:, :]), heads(chunk(v.tok, c, slice(VAL, VAL + D_MODEL))), per_head(v.w_st, c, r), ALU.mult)\
                    .then_inc(s["xw_ready"], 1)

            def sum_state(c, r, q):
                ch.link(tt(heads(state[:, :]), heads(state[:, :]), per_head(v.e_tot, c, r), ALU.mult))
                tt(state[:, :], state[:, :], Xf[q], ALU.add).then_inc(x_free[q], 1)

            def from_ctx(r, cs, jobs):
                for m, c in enumerate(cs):
                    weigh(c, r)
                    dve.wait_ge(s["x_done"], jobs + m + 1)
                    if m == 0:
                        dve.tensor_copy(state[:, :], Xf[0]).then_inc(x_free[0], 1)
                        dve.wait_ge(x_free[0], (jobs + 2) // 2)
                    else:
                        sum_state(c, r, m)
                        dve.wait_ge(x_free[m], (jobs + 2) // 2)

            from_ctx(1, (ALL_C - 1, ALL_C - 2), 0)
            with dve.Fori(0, NC) as i:
                ch.enter(i, 3)
                c = NC - 1 - i
                values = heads(chunk(v.tok, c, slice(VAL, VAL + D_MODEL)))
                weigh(c, 1)
                dve.wait_ge(s["y_out"], 16 * i)
                ch.link(tt(heads(y[:, :]), values, bc(v.rows[:, 64:64 + SSM_HEADS], 2, HDIM), ALU.mult))
                dve.wait_ge(s["x_done"], back + BWD_JOBS * i + 1)
                tmp = E[:, 1, :]
                tt(heads(tmp), heads(Xf[0]), per_head(v.e_acs, c, 1), ALU.mult).then_inc(x_free[0], 1)
                dve.wait_ge(x_free[0], back // 2 + i + 1)
                ch.link(tt(y[:, :], y[:, :], tmp, ALU.add))
                dve.sem_inc(s["y_ready"], 1)
                dve.wait_ge(s["x_done"], back + BWD_JOBS * i + 2)
                sum_state(c, 1, 1)
                dve.wait_ge(x_free[1], back // 2 + i + 1)
                ch.leave(NC)
            from_ctx(0, (NC, NC + 1), fwd_ctx)
            with dve.Fori(0, NC) as i:
                ch.enter(i, 10)

                def done(j):
                    dve.wait_ge(s["x_done"], fwd + J * i + j + 1)

                def freed(j):
                    dve.wait_ge(x_free[j % 2], (fwd + j) // 2 + i * (J // 2) + 1)

                def group(buf, r, g):
                    at = SSM_HEADS * r + HPG * g
                    return bc(chunk(buf, i, slice(at, at + HPG)), 2, P)

                def between(r, g):
                    tt(lhs[r][:, :].rearrange("p (h t) -> p h t", h=HPG),
                       bc(k.mats[:, (TRI_GT, TRI_LT)[r], :], 1, HPG), group(v.dta, r, g), ALU.mult)\
                        .then_inc(s["lhs_ready"], 1)

                def weights(g):
                    for r, e, j in ((0, 2 * g, (F0, F1)[g]), (1, 1, (B0, B1)[g])):
                        ev = E[:, e, :].rearrange("p (h t) -> p h t", h=HPG)
                        freed(j)
                        ch.link(tt(ev, ev, group(v.dt, r, g), ALU.mult))
                        ch.link(tt(ev, ev, bc(cbm[:, r, g, :], 1, HPG), ALU.mult))
                    tt(E[:, 2 * g, :], E[:, 2 * g, :], E[:, 1, :], ALU.add).then_inc(s["w_ready"], 1)

                between(0, 0)
                between(1, 0)
                done(CB)
                cb = X[0][:, 0, 0:NGRP * P].rearrange("p (g t) -> p g t", g=NGRP)
                ch.link(tt(cbm[:, 0, :, :], cb, bc(k.mats[:, TRI_LE, :], 1, NGRP), ALU.mult))
                tt(cbm[:, 1, :, :], cb, bc(k.mats[:, TRI_GE, :], 1, NGRP), ALU.mult).then_inc(x_free[0], 1)
                freed(CB)
                done(OFF)
                tmp = E[:, 1, :]
                tt(heads(tmp), heads(Xf[1]), per_head(v.e_acs, i, 0), ALU.mult).then_inc(x_free[1], 1)
                freed(OFF)
                dve.wait_ge(s["y_in"], 16 * (i + 1))
                tt(y[:, :], y[:, :], tmp, ALU.add).then_inc(s["off_added"], 1)
                dve.wait_ge(s["off_added"], i + 1)
                done(F0)
                between(0, 1)
                done(B0)
                between(1, 1)
                weights(0)
                dve.wait_ge(s["w_ready"], 2 * i + 1)
                done(B1)
                weigh(i, 0)
                weights(1)
                done(ST)
                sum_state(i, 0, 0)
                done(DIAG)
                tt(y[:, :], y[:, :], Xf[1], ALU.add).then_inc(x_free[1], 1)
                freed(DIAG)
                dve.sem_inc(s["y_ready"], 1)
                ch.leave(NC)


def phase6(nc, k, d, w):
    with ExitStack() as ctx:
        s = signals(nc, ctx, "p6", "y_in z_in x_done x_free0 x_free1 sq added sums root inv row raw hi lo cleared u_in0 "
                                   "u_in1 area_in pooled ghi glo pm phi plo x_in chain")
        r1, r2 = signals(nc, ctx, "p6r", NORM), signals(nc, ctx, "p6n", NORM)
        X, Xf = aux(k)
        pair = [k.ps[:, 2 * q:2 * q + 2, :].rearrange("p a b -> p (a b)") for q in range(2)]
        x_free, u_in = [s["x_free0"], s["x_free1"]], [s["u_in0"], s["u_in1"]]
        ident = k.mats[:, IDENT, :]
        PG = KT // NGRP
        FIRST = KT // 2
        Y0, POOL0, PM0 = UZ_END, UZ_END + KT, UZ_END + KT + 2
        EDGE = max(WINDOWS) // 2
        flat = w.x[:, :, :].rearrange("p a b -> p (a b)")
        R_ = (ROWS + 2 * EDGE) * GRID_W
        C_ = ROWS * (GRID_W + 2 * EDGE)
        u_pad = [flat[:, q * R_:(q + 1) * R_].rearrange("p (r c) -> p r c", c=GRID_W) for q in range(2)]
        sums_r = flat[:, 2 * R_:3 * R_].rearrange("p (r c) -> p r c", c=GRID_W)
        sums_c = flat[:, 2 * R_:2 * R_ + C_].rearrange("p (r c) -> p r c", r=ROWS)
        c_pad = flat[:, 3 * R_:3 * R_ + C_].rearrange("p (r c) -> p r c", r=ROWS)
        pooled = c_pad[:, :, EDGE:EDGE + GRID_W]
        area = w.acc[:, :].rearrange("p (r c) -> p r c", r=ROWS)
        vec = lambda name, t: k.vecs[:, VEC[name][0] + t:VEC[name][0] + t + 1]
        block = ctx.enter_context(nc.Block())

        @block.sync
        def _(sp):
            sp.dma_start(w.x[:, :, :], d.y_tok.rearrange("c p n -> p c n")).then_inc(s["y_in"], 16)
            sp.dma_start(w.mix[:, :, :], d.z_scr.rearrange("t p n -> p t n")).then_inc(s["z_in"], 16)
            stream_load(sp, k, UZ_END + 4, OUT2_END + 4)

        @block.gpsimd
        def _(pool):
            stream_split(pool, k, UZ_END + 2, OUT2_END + 2)

        @block.tensor
        def _(pe):
            pe.wait_ge(s["y_in"], 16)
            for t in range(KT):
                if t >= 2:
                    pe.wait_ge(x_free[t % 2], t // 2)
                for c in range(NC):
                    ins = pe.transpose(Xf[t % 2][:, c * P:(c + 1) * P], w.x[:, c, t * P:(t + 1) * P], ident)
                ins.then_inc(s["x_done"], 1)
            for g in range(NGRP):
                pe.wait_ge(s["added"], PG * (g + 1))
                for c in range(NC):
                    ins = pe.matmul(pair[g][:, c:c + 1], w.acc[:, c * P:(c + 1) * P], k.mean_col[:, :],
                                    start=True, stop=True)
                ins.then_inc(s["sums"], 1)
            for g in range(NGRP):
                pe.wait_ge(s["inv"], g + 1)
                for c in range(NC):
                    ins = pe.matmul(pair[g][:, c * P:(c + 1) * P], w.rcol[:, c:c + 1].broadcast_to([P, P]), ident,
                                    start=True, stop=True)
                ins.then_inc(s["row"], 1)
            pe.wait_ge(s["lo"], KT)
            with pe.Fori(0, KT // 2) as j:
                for q in range(2):
                    gemm(pe, k, Y0 + 2 * j + q, q, Y0 // 2 + j, w.a_hi, w.a_lo)
            for p in range(2):
                pe.wait_ge(s["glo"], FIRST * (p + 1))
                pe.wait_ge(k.w_split, POOL0 + p + 1)
                for e in range(FIRST):
                    t = FIRST * p + e
                    pe.wait_ge(x_free[t % 2], (KT + t) // 2)
                    ins = tile_products(pe, k, p, w.g_hi, w.g_lo,
                                        [(X[t % 2][:, h, :], slice(h * HALF, (h + 1) * HALF)) for h in range(2)],
                                        kts=2, at=e * 2 * P, kt0=e // 2 * 2)
                    if e < FIRST - 1:
                        ins.then_inc(s["x_done"], 1)
                ins.then_inc(k.tile_done, 1)
            pe.wait_ge(s["plo"], KT)
            with pe.Fori(0, KT // 2) as j:
                for q in range(2):
                    gemm(pe, k, PM0 + 2 * j + q, q, PM0 // 2 + j, w.a_hi, w.a_lo)
            rstd_pe(pe, k, w, r1)
            rstd_pe(pe, k, w, r2)

        def pool_products_done(eng, t):
            p, e = t // FIRST, t % FIRST
            if e < FIRST - 1:
                eng.wait_ge(s["x_done"], KT + p * (FIRST - 1) + e + 1)
            else:
                eng.wait_ge(k.tile_done, POOL0 + p + 1)

        @block.scalar
        def _(act):
            for t in range(KT):
                act.wait_ge(x_free[t % 2], t // 2 + 1)
                if t >= 2:
                    act.wait_ge(s["added"], t - 1)
                act.activation(w.tmp[:, t % 2, :], w.mix[:, t, :], ACT.Square).then_inc(s["sq"], 1)
            for g in range(NGRP):
                act.wait_ge(s["sums"], g + 1)
                if g:
                    act.wait_ge(s["inv"], g)
                act.activation(w.col[:, :], pair[g][:, 0:NC], ACT.Sqrt, bias=k.eps[:, :], scale=1.0 * NGRP)\
                   .then_inc(s["root"], 1)
            act.wait_ge(s["cleared"], 1)

            def load_u(t):
                act.dma_start(u_pad[t % 2][:, EDGE:EDGE + ROWS, :],
                              d.u_scr[t, :, :].rearrange("p (r c) -> p r c", r=ROWS)).then_inc(u_in[t % 2], 16)

            def load_area(i):
                act.dma_start(w.acc[:, :], d.pool_area[i, :, :]).then_inc(s["area_in"], 16)

            load_u(0)
            load_u(1)
            act.wait_ge(s["sums"], NGRP)
            load_area(0)
            for t in range(KT):
                act.wait_ge(s["raw"], t + 1)
                act.activation(w.a_hi[:, t, :], w.tmp[:, t % 2, :], ACT.Copy).then_inc(s["hi"], 1)

            def pooled_high(t):
                act.wait_ge(s["pooled"], t + 1)
                if t >= FIRST:
                    act.wait_ge(k.tile_done, POOL0 + 1)
                act.activation(w.g_hi[:, t % FIRST, :].rearrange("p (r c) -> p r c", r=ROWS), pooled, ACT.Copy)\
                   .then_inc(s["ghi"], 1)
                act.wait_ge(s["glo"], t + 1)
                if t + 2 < KT:
                    load_u(t + 2)
                if t % 2 and t < KT - 1:
                    load_area(t // 2 + 1)

            for t in range(FIRST):
                pooled_high(t)
                for q in range(2):
                    act.wait_ge(k.tile_done, Y0 + 2 * t + q + 1)
                    act.activation(w.mix[:, 2 * t + q, :], pair[q], ACT.Copy).then_inc(k.pair_free[q], 1)

            def mixed_high(p):
                for e in range(FIRST):
                    t = FIRST * p + e
                    act.wait_ge(s["pm"], t + 1)
                    act.activation(w.a_hi[:, t, :], w.tmp[:, t % 2, :], ACT.Copy).then_inc(s["phi"], 1)

            mixed_high(0)
            for t in range(FIRST, KT):
                pooled_high(t)
            act.dma_start(w.x[:, :, :], d.x2_scr).then_inc(s["x_in"], 16)
            mixed_high(1)
            squares_act(act, w, r1, w.mix, lambda t: act.wait_ge(k.pair_free[t % 2], PM0 // 2 + t // 2 + 1))
            root_act(act, k, w, r1)
            squares_act(act, w, r2, w.x, lambda t: act.wait_ge(r1["x_new"], t + 1))
            root_act(act, k, w, r2)
            split_norm_act(act, w, r2, lambda t: k.mod[:, MOD_B2, t:t + 1])

        @block.vector
        def _(dve):
            ch = Chain(dve, s["chain"])
            tt, ts, stt = dve.tensor_tensor, dve.tensor_scalar, dve.scalar_tensor_tensor

            def add(t):
                dve.wait_ge(s["sq"], t + 1)
                if t % PG == 0:
                    if t:
                        dve.wait_ge(s["sums"], t // PG)
                    dve.tensor_copy(w.acc[:, :], w.tmp[:, t % 2, :]).then_inc(s["added"], 1)
                else:
                    dve.wait_ge(s["added"], t)
                    tt(w.acc[:, :], w.acc[:, :], w.tmp[:, t % 2, :], ALU.add).then_inc(s["added"], 1)

            dve.wait_ge(s["z_in"], 16)
            for t in range(KT):
                dve.wait_ge(s["x_done"], t + 1)
                tt(w.mix[:, t, :], w.mix[:, t, :], Xf[t % 2], ALU.mult).then_inc(x_free[t % 2], 1)
                if t:
                    add(t - 1)
            add(KT - 1)
            dve.memset(flat, 0.0).then_inc(s["cleared"], 1)
            for g in range(NGRP):
                dve.wait_ge(s["root"], g + 1)
                if g:
                    dve.wait_ge(s["row"], g)
                dve.reciprocal(w.rcol[:, :], w.col[:, :]).then_inc(s["inv"], 1)
            dve.wait_ge(s["row"], NGRP)

            def low(t):
                dve.wait_ge(s["hi"], t + 1)
                tt(w.a_lo[:, t, :], w.tmp[:, t % 2, :], w.a_hi[:, t, :].bitcast(F32), ALU.subtract).then_inc(s["lo"], 1)

            for t in range(KT):
                if t >= 2:
                    dve.wait_ge(s["lo"], t - 1)
                stt(out=w.tmp[:, t % 2, :], in0=w.mix[:, t, :], scalar=vec("ssm_norm", t), in1=pair[t // PG],
                    op0=ALU.mult, op1=ALU.mult).then_inc(s["raw"], 1)
                if t:
                    low(t - 1)
            low(KT - 1)

            def pool_tile(t):
                width = WINDOWS[t // 2]
                at = EDGE - width // 2
                dve.wait_ge(u_in[t % 2], 16 * (t // 2 + 1))
                if t:
                    dve.wait_ge(s["glo"], t)
                else:
                    dve.wait_ge(s["cleared"], 1)

                def doubling(src, part, n, last):
                    span = 1
                    while span < width:
                        size = n + width - 2 * span
                        dst = sums if 2 * span < width else last
                        start = at if dst is not last or last is sums else EDGE
                        ch.link(tt(part(dst, start, size), part(src, at, size), part(src, at + span, size), ALU.add))
                        src, span = sums, 2 * span

                sums = sums_r
                doubling(u_pad[t % 2], lambda b, a, n: b[:, a:a + n, :] if b is not c_pad else pooled[:, :, :],
                         ROWS, c_pad)
                sums = sums_c
                doubling(c_pad, lambda b, a, n: b[:, :, a:a + n], GRID_W, sums_c)
                if t % 2 == 0:
                    dve.wait_ge(s["area_in"], 16 * (t // 2 + 1))
                ch.link(tt(pooled, sums_c[:, :, at:at + GRID_W], area, ALU.mult))
                tt(pooled, pooled, u_pad[t % 2][:, EDGE:EDGE + ROWS, :], ALU.subtract).then_inc(s["pooled"], 1)

            def pooled_low(t):
                dve.wait_ge(s["ghi"], t + 1)
                lo, hi = (g[:, t % FIRST, :].rearrange("p (r c) -> p r c", r=ROWS) for g in (w.g_lo, w.g_hi))
                tt(lo, pooled, hi.bitcast(F32), ALU.subtract).then_inc(s["glo"], 1)

            def mixed_low(t):
                dve.wait_ge(s["phi"], t + 1)
                tt(w.a_lo[:, t, :], w.tmp[:, t % 2, :], w.a_hi[:, t, :].bitcast(F32), ALU.subtract).then_inc(s["plo"], 1)

            def mixed(p):
                for e in range(FIRST):
                    t = FIRST * p + e
                    pool_products_done(dve, t)
                    if t >= 2:
                        dve.wait_ge(s["plo"], t - 1)
                    ts(w.tmp[:, t % 2, :], Xf[t % 2], vec("pool_scale", t), None, ALU.mult).then_inc(x_free[t % 2], 1)
                    dve.wait_ge(x_free[t % 2], (KT + t) // 2 + 1)
                    dve.sem_inc(s["pm"], 1)
                    if e:
                        mixed_low(t - 1)
                mixed_low(FIRST * p + FIRST - 1)
                dve.sem_inc(k.pair_free[p], 1)

            for t in range(FIRST):
                pool_tile(t)
                pooled_low(t)
            pool_tile(FIRST)
            mixed(0)
            pooled_low(FIRST)
            for t in range(FIRST + 1, KT):
                pool_tile(t)
                pooled_low(t)
            mixed(1)
            for t in range(KT):
                dve.wait_ge(k.tile_done, PM0 + t + 1)
                tt(w.mix[:, t, :], w.mix[:, t, :], pair[t % 2], ALU.add).then_inc(k.pair_free[t % 2], 1)
                if t:
                    add_square(dve, w, r1, t - 1)
            add_square(dve, w, r1, KT - 1)
            inverse_dve(dve, w, r1)
            dve.wait_ge(s["x_in"], 16)
            residual_dve(dve, k, w, r1, ch, lambda t: k.mod[:, MOD_G1, t:t + 1],
                         lambda t: add_square(dve, w, r2, t - 1) if t else None)
            add_square(dve, w, r2, KT - 1)
            inverse_dve(dve, w, r2)
            split_norm_dve(dve, k, w, r2, lambda t: k.mod[:, MOD_A2, t:t + 1], lambda t: k.mod[:, MOD_B2, t:t + 1])


class Dram:
    pass


def clear_semaphores(nc):
    with nc.Block() as block:
        @block.gpsimd
        def _(pool):
            left = sorted(set(nc.released_uncleared_semaphores))
            while left:
                first = last = left.pop(0)
                while left and left[0] == last + 1:
                    last = left.pop(0)
                pool.sem_clear(range(first, last + 1))


def build(nc, arrays, out):
    d = Dram()
    d.rope, d.head_consts, d.mats, d.pool_area = (arrays[n] for n in ("rope", "head_consts", "mats", "pool_area"))
    d.wstream, d.ada_w, d.w_dt = (arrays[n] for n in ("wstream", "ada_w", "w_dt"))
    d.xT, d.ctxT, d.vecs, d.prm = (arrays[n] for n in ("xT", "ctxT", "vecs", "prm"))
    d.d_rows, d.head_rows = arrays["d_rows"], arrays["head_rows"]

    def scratch(name, shape):
        return nc.dram_tensor(name, shape, F32, kind="Internal").ap()

    d.y_scr = scratch("mixer_out", [2 * HEADS, P, SEQ])
    d.x2_scr = scratch("x_block2", [P, KT, SEQ])
    d.u_scr, d.z_scr = scratch("u_rows", [KT, P, SEQ]), scratch("z_rows", [KT, P, SEQ])
    d.y_tok = scratch("y_by_token", [NC, P, D_MODEL])
    with ExitStack() as ctx:
        k = open_kit(nc, ctx, d)
        phase1(nc, k, d)
        with ExitStack() as half:
            w = open_work(nc, half, "b1")
            phase2(nc, k, d, w)
            mlp_phase(nc, k, d, w, P1_TILES + P2_TILES,
                      lambda t: k.vecs[:, VEC["mlp_post"][0] + t:VEC["mlp_post"][0] + t + 1], "m1",
                      ada_from=4 * HEADS, out=d.x2_scr)
        with ExitStack() as half:
            clear_semaphores(nc)
            v = open_scan(nc, half)
            phase4(nc, k, d, v)
            phase5(nc, k, d, v)
        with ExitStack() as half:
            clear_semaphores(nc)
            w = open_work(nc, half, "b2")
            phase6(nc, k, d, w)
            mlp_phase(nc, k, d, w, OUT2_END, lambda t: k.mod[:, MOD_G2, t:t + 1], "m2", out=out)




def tile_of(w, m, rows=slice(None)):
    w = w[rows, m * P:(m + 1) * P]
    return w.reshape(-1, P, P).transpose(1, 0, 2).reshape(P, -1)


def weight_stream(a):
    w_in, glu, w_out = a["w_in"][0], a["w_glu"][0], a["w_out"][0]
    w_in2, w_out2, pool_w = a["w_in_2"][0], a["w_out_2"][0], a["pool_w_2"][0]
    out = []
    q0, k0, v0, g0, u0 = (4 * j for j in range(5))
    for i in range(HEADS):
        out += [tile_of(w_in, c + i) for c in (u0, k0, v0, q0, g0)]
    out += [np.concatenate([tile_of(glu, 4 + i), tile_of(glu, i)], axis=1) for i in range(GLU_TILES)]
    out += [tile_of(w_out, m) for m in range(KT)]

    def mlp(w1, w2):
        for b in range(MLP_STEPS):
            for m in range(HID):
                yield tile_of(w1, b * HID + m)
            rows = slice(b * HID * P, (b + 1) * HID * P)
            for m in range(KT // 2):
                yield np.concatenate([tile_of(w2, 2 * m, rows), tile_of(w2, 2 * m + 1, rows)], axis=1)

    out += mlp(a["w_ff1"][0], a["w_ff2"][0])
    out += [tile_of(w_in2, m) for m in (16, 17, 18, 19, 8, 9, 10, 11, 12, 13, 14, 15)]
    u2 = w_in2[:, 2592:3616]
    for m in range(KT):
        out += [tile_of(u2, m), tile_of(w_in2, m)]
    pool = [[tile_of(pool_w[g], m) for m in range(2)] for g in range(4)]
    out += [tile_of(w_out2, m, slice(0, 1024)) for m in range(KT)]
    out += [np.concatenate(pool[0] + pool[1], axis=1), np.concatenate(pool[2] + pool[3], axis=1)]
    out += [tile_of(w_out2, m, slice(1024, 2048)) for m in range(KT)]
    out += mlp(a["w_mlp1_2"][0], a["w_mlp2_2"][0])
    assert len(out) == ALL_TILES
    return np.ascontiguousarray(np.stack(out))


def columns(v):
    return np.asarray(v).reshape(-1, P).T


def shape_constants():
    f = np.float32
    c = {}
    half = HEAD_DIM // 2
    inv = (f(10000.0) ** (-np.arange(half, dtype=f) / f(half))).astype(f)
    angle = (np.arange(SEQ, dtype=f)[:, None] * inv[None, :]).astype(f).astype(np.float64).T
    cos, sin = np.cos(angle), np.sin(angle)
    c["rope"] = np.stack([np.concatenate([cos, cos]), np.concatenate([-sin, sin])]).astype(f)
    lg = np.log(1.0 - np.exp(np.linspace(math.log(1.0 / 32), math.log(1.0 / 512), HEADS).astype(f).astype(np.float64)))
    lg = lg.astype(f).astype(np.float64)
    idx = np.arange(P, dtype=np.float64)
    scale = HEAD_DIM ** -0.5
    hcs = np.zeros((HEADS + 1, P, HC_COLS), f)
    for h in range(HEADS):
        diff = idx[None, :] - idx[:, None]
        hcs[h, :, HC_DECAY:HC_DECAY + P] = np.where(diff >= 0, np.exp(np.maximum(diff, 0) * lg[h]), 0.0) * scale
        hcs[h, :, HC_XI:HC_XI + P] = np.exp((idx + 1) * lg[h])[None, :]
        hcs[h, :, HC_ZETA] = np.exp((P - 1 - idx) * lg[h]) * scale
        hcs[h, :, HC_GAMMA] = np.exp(P * lg[h])
    c["head_consts"] = hcs
    mats = np.zeros((6, P, P), f)
    mats[IDENT] = np.eye(P)
    mats[CENTER] = np.eye(P) - 1.0 / P
    mats[TRI_LE] = idx[:, None] <= idx[None, :]
    mats[TRI_GE] = idx[:, None] >= idx[None, :]
    mats[TRI_GT] = idx[:, None] > idx[None, :]
    mats[TRI_LT] = idx[:, None] < idx[None, :]
    c["mats"] = mats
    counts = []
    for w in WINDOWS:
        def n(length):
            t = np.arange(length)
            return np.clip(t + w // 2, 0, length) - np.clip(t - w // 2, 0, length)
        counts.append((1.0 / (n(ROWS)[:, None] * n(GRID_W)[None, :])).reshape(-1))
    c["pool_area"] = np.ascontiguousarray(np.broadcast_to(np.array(counts, f)[:, None, :], (4, P, SEQ)))
    return c


def lay_out(a):
    a = {name: np.asarray(v) for name, v in a.items()}
    o = shape_constants()
    o["wstream"] = weight_stream(a)
    o["ada_w"] = np.stack([tile_of(a["w_ada_2"][0], m) for m in range(48)] + [tile_of(a["w_ada_2"][0], 47)])
    o["xT"] = np.ascontiguousarray(a["x"][0].T.reshape(KT, P, SEQ).transpose(1, 0, 2))
    o["ctxT"] = np.ascontiguousarray(a["ctx_2"][0].T.reshape(KT, P, CTX).transpose(1, 0, 2))
    taps = a["conv_w_2"][0].T.reshape(XBC_TILES, P, TAPS).transpose(1, 0, 2)
    order = [8, 9, 10, 11, 0, 1, 2, 3, 4, 5, 6, 7]
    conv_b = columns(a["conv_b_2"][0])
    cc = np.stack([columns(a["c_2"][0]), columns(a["c_ctx_2"])], axis=2)
    parts = [columns(a[n][0]) for n in ("norm_mix_pre", "norm_mix_post", "norm_mlp_pre", "norm_mlp_post", "ret_gn_gain",
                                        "pre_mix_g_2", "post_mix_g_2", "pre_mlp_g_2", "post_mlp_g_2", "ssm_norm_w_2",
                                        "pool_scale_2")]
    parts += [taps[:, order, :].reshape(P, -1), conv_b[:, order], columns(a["b_ada_2"][0]), cc.reshape(P, -1)]
    o["vecs"] = np.ascontiguousarray(np.concatenate(parts, axis=1))

    def by_state(v):
        v = v.reshape(FT, GT, 2 * STATE, *v.shape[2:])
        return np.moveaxis(v, 1, 2).reshape(FT, P, -1)
    ldt = np.broadcast_to(a["ssm_log_dt"][0][:, None], (GROUPS, STATE))
    prm = np.concatenate([by_state(v) for v in (
        a["ssm_lambda_re"][0], a["ssm_lambda_im"][0], ldt, a["ssm_b_re"][0], a["ssm_b_im"][0],
        a["ssm_c_re"][0].transpose(0, 2, 1), a["ssm_c_im"][0].transpose(0, 2, 1))], axis=2)
    o["prm"] = np.concatenate([prm, prm[-1:]], axis=0)
    o["d_rows"] = np.ascontiguousarray(a["ssm_d"][0].reshape(GROUPS, GROUP_CH).T)
    w_dt = a["w_in_2"][0][:, 2560:2592]
    o["w_dt"] = np.ascontiguousarray(w_dt.reshape(KT, P, 32).transpose(1, 0, 2))
    row = np.concatenate([a["dt_bias_2"][0].reshape(-1), a["a_log_2"][0].reshape(-1), a["d_skip_2"][0]])
    o["head_rows"] = np.ascontiguousarray(np.broadcast_to(row, (P, row.size)))
    return o


def kernel(**inputs):
    import concourse.bacc as bacc
    from concourse.bass_utils import run_bass_kernel_spmd

    nc = bacc.Bacc("TRN2", target_bir_lowering=False, num_devices=1)
    laid = lay_out(inputs)
    arrays = {name: nc.dram_tensor(f"in_{name}", v.shape, mybir.dt.from_np(v.dtype), kind="ExternalInput").ap()
              for name, v in laid.items()}
    out = nc.dram_tensor("out_x", [P, KT, SEQ], F32, kind="ExternalOutput").ap()
    build(nc, arrays, out)
    result = run_bass_kernel_spmd(nc, [{f"in_{name}": v for name, v in laid.items()}], core_ids=[0])
    by_feature = result.results[0]["out_x"]
    return np.ascontiguousarray(by_feature.transpose(1, 0, 2).reshape(D_MODEL, SEQ).T)[None]
```
